# Optimizing a Trainium2 kernel written in Bass

```python
import jax, jax.numpy as jnp
from jax import lax
import numpy as np

D_MODEL = 1024
BATCH = 1
SEQ = 512
DEPTH = 2

ML_HEADS = 4
ML_DQK = 64
ML_DV = 128
ML_CONV = 4
ML_CHUNK = 64
MOBA_HEADS = 4
MOBA_DH = 64
MOBA_BLOCK = 256
MOBA_TOPK = 3
MOBA_QCHUNK = 64
DSA_HEADS = 4
DSA_DH = 64
IDX_HEADS = 4
IDX_DH = 64
DSA_TOPK_MAX = 256
DSA_QCHUNK = 128
D_FF = 4 * D_MODEL
EPS = 1e-6

ML_QK_W = ML_HEADS * ML_DQK
ML_V_W = ML_HEADS * ML_DV
MOBA_W = MOBA_HEADS * MOBA_DH
DSA_W = DSA_HEADS * DSA_DH
D_MIX = ML_V_W + MOBA_W + DSA_W
IN_SPLITS = (ML_QK_W, ML_QK_W, ML_V_W, ML_V_W, ML_HEADS, ML_HEADS,
             MOBA_W, MOBA_W, MOBA_W,
             DSA_W, DSA_W, DSA_W, IDX_HEADS * IDX_DH, IDX_DH, IDX_HEADS)
D_IN = 2 * ML_QK_W + 2 * ML_V_W + 2 * ML_HEADS + 3 * MOBA_W + 3 * DSA_W + IDX_HEADS * IDX_DH + IDX_DH + IDX_HEADS

kernel_name = 'hybrid_mlstm_moba_dsa_trunk'

def _split_points():
    pts, acc = [], 0
    for n in IN_SPLITS[:-1]:
        acc += n
        pts.append(acc)
    return pts

def rmsnorm(x, g):
    xf = x.astype(jnp.float32)
    y = xf * lax.rsqrt(jnp.mean(xf * xf, axis=-1, keepdims=True) + EPS)
    return (y * g.astype(jnp.float32)).astype(x.dtype)

def causal_conv(x, w):
    K = w.shape[0]
    S = x.shape[1]
    xp = jnp.pad(x, ((0, 0), (K - 1, 0), (0, 0)))
    return sum(xp[:, j:j + S] * w[j] for j in range(K))

def mlstm_chunkwise(q, k, v, ig, fg):
    B, H, S, DK = q.shape
    DV = v.shape[-1]
    L = ML_CHUNK
    NC = S // L
    q = q.reshape(B, H, NC, L, DK) * (DK ** -0.5)
    k = k.reshape(B, H, NC, L, DK)
    v = v.reshape(B, H, NC, L, DV)
    ig = ig.reshape(B, H, NC, L)
    lf = jax.nn.log_sigmoid(fg).reshape(B, H, NC, L)
    b = jnp.cumsum(lf, axis=-1)
    causal = jnp.tril(jnp.ones((L, L), dtype=bool))
    dlog = jnp.where(causal, b[..., :, None] - b[..., None, :] + ig[..., None, :], -jnp.inf)
    bL = b[..., -1]
    a = bL[..., None] - b + ig
    m_loc = jnp.max(a, axis=-1)
    wa = jnp.exp(a - m_loc[..., None])
    C_loc = jnp.einsum('bhcs,bhcsv,bhcsk->bhcvk', wa, v, k)
    n_loc = jnp.einsum('bhcs,bhcsk->bhck', wa, k)

    def step(carry, xs):
        C, n, m = carry
        bL_c, m_c, C_c, n_c = xs
        m_new = jnp.maximum(bL_c + m, m_c)
        s_old = jnp.exp(bL_c + m - m_new)
        s_loc = jnp.exp(m_c - m_new)
        C_new = s_old[..., None, None] * C + s_loc[..., None, None] * C_c
        n_new = s_old[..., None] * n + s_loc[..., None] * n_c
        return (C_new, n_new, m_new), (C, n, m)

    init = (jnp.zeros((B, H, DV, DK), jnp.float32), jnp.zeros((B, H, DK), jnp.float32),
            jnp.zeros((B, H), jnp.float32))
    xs = (jnp.moveaxis(bL, 2, 0), jnp.moveaxis(m_loc, 2, 0),
          jnp.moveaxis(C_loc, 2, 0), jnp.moveaxis(n_loc, 2, 0))
    _, (C0, n0, m0) = lax.scan(step, init, xs)
    C0 = jnp.moveaxis(C0, 0, 2)
    n0 = jnp.moveaxis(n0, 0, 2)
    m0 = jnp.moveaxis(m0, 0, 2)
    inter = b + m0[..., None]
    m_t = jnp.maximum(inter, jnp.max(dlog, axis=-1))
    w_inter = jnp.exp(inter - m_t)
    w_intra = jnp.exp(dlog - m_t[..., None]) * jnp.einsum('bhcjk,bhcsk->bhcjs', q, k)
    num = w_inter[..., None] * jnp.einsum('bhcvk,bhcjk->bhcjv', C0, q) + jnp.einsum('bhcjs,bhcsv->bhcjv', w_intra, v)
    den = w_inter * jnp.einsum('bhck,bhcjk->bhcj', n0, q) + jnp.sum(w_intra, axis=-1)
    h = num / jnp.maximum(jnp.abs(den), jnp.exp(-m_t))[..., None]
    return h.reshape(B, H, S, DV)

def mlstm_group(q, k, v, o, ig, fg, conv_w, head_norm):
    B, S, _ = q.shape
    f32 = jnp.float32
    qk = jax.nn.silu(causal_conv(jnp.concatenate([q, k], axis=-1).astype(f32), conv_w.astype(f32)))
    q, k = qk[..., :ML_QK_W], qk[..., ML_QK_W:]
    heads = lambda t, d: t.reshape(B, S, ML_HEADS, d).transpose(0, 2, 1, 3)
    h = mlstm_chunkwise(heads(q, ML_DQK), heads(k, ML_DQK), heads(v.astype(f32), ML_DV),
                        ig.astype(f32).transpose(0, 2, 1), fg.astype(f32).transpose(0, 2, 1))
    h = h.transpose(0, 2, 1, 3)
    h = h * lax.rsqrt(jnp.mean(h * h, axis=-1, keepdims=True) + EPS)
    h = h.reshape(B, S, ML_V_W) * head_norm.astype(f32)
    return (jax.nn.sigmoid(o.astype(f32)) * h).astype(v.dtype)

def moba_group(q, k, v):
    B, S, _ = q.shape
    H, D, BS = MOBA_HEADS, MOBA_DH, MOBA_BLOCK
    NB = -(-S // BS)
    pad = NB * BS - S
    q = q.reshape(B, S, H, D).transpose(0, 2, 1, 3)
    k = k.reshape(B, S, H, D).transpose(0, 2, 1, 3)
    v = v.reshape(B, S, H, D).transpose(0, 2, 1, 3)
    kb = jnp.pad(k, ((0, 0), (0, 0), (0, pad), (0, 0))).reshape(B, H, NB, BS, D)
    vb = jnp.pad(v, ((0, 0), (0, 0), (0, pad), (0, 0))).reshape(B, H, NB, BS, D)
    k_mean = jnp.mean(kb.astype(jnp.float32), axis=3)
    n_sel = max(min(MOBA_TOPK, NB - 1), 1)
    QC = MOBA_QCHUNK
    NQ = S // QC
    qc = q.reshape(B, H, NQ, QC, D).transpose(2, 0, 1, 3, 4)
    bidx = jnp.arange(B)[:, None, None, None]
    hidx = jnp.arange(H)[None, :, None, None]

    def chunk(args):
        qi, ci = args
        t = ci * QC + jnp.arange(QC)
        own = t // BS
        gate = jnp.einsum('bhqd,bhnd->bhqn', qi.astype(jnp.float32), k_mean)
        past = jnp.arange(NB)[None, :] < own[:, None]
        gate = jnp.where(past, gate, -jnp.inf)
        _, sel = lax.top_k(gate, n_sel)
        blocks = jnp.concatenate([sel, jnp.broadcast_to(own[:, None], (B, H, QC, 1))], axis=-1)
        blk_ok = jnp.concatenate([sel < own[:, None], jnp.ones((B, H, QC, 1), dtype=bool)], axis=-1)
        kg = kb[bidx, hidx, blocks]
        vg = vb[bidx, hidx, blocks]
        s = jnp.einsum('bhqd,bhqnkd->bhqnk', qi, kg).astype(jnp.float32) * (D ** -0.5)
        kpos = blocks[..., None] * BS + jnp.arange(BS)
        mask = blk_ok[..., None] & (kpos <= t[:, None, None])
        s = jnp.where(mask, s, -jnp.inf).reshape(B, H, QC, -1)
        p = jax.nn.softmax(s, axis=-1).reshape(kg.shape[:-1]).astype(v.dtype)
        return jnp.einsum('bhqnk,bhqnkd->bhqd', p, vg)

    out = lax.map(chunk, (qc, jnp.arange(NQ)))
    return out.transpose(1, 0, 3, 2, 4).reshape(B, S, H * D)

def dsa_group(q, k, v, iq, ik, iw):
    B, S, _ = q.shape
    H, D = DSA_HEADS, DSA_DH
    topk = min(DSA_TOPK_MAX, S // 4)
    QC = DSA_QCHUNK
    NQ = S // QC
    qh = q.reshape(B, NQ, QC, H, D).transpose(1, 0, 2, 3, 4)
    kh = k.reshape(B, S, H, D)
    vh = v.reshape(B, S, H, D)
    iqc = iq.reshape(B, NQ, QC, IDX_HEADS, IDX_DH).transpose(1, 0, 2, 3, 4)
    iwc = (iw.astype(jnp.float32) * (IDX_HEADS ** -0.5 * IDX_DH ** -0.5)).reshape(B, NQ, QC, IDX_HEADS).transpose(1, 0, 2, 3)
    bidx = jnp.arange(B)[:, None, None]

    def chunk(args):
        qi, iqi, iwi, ci = args
        t = ci * QC + jnp.arange(QC)
        rel = jax.nn.relu(jnp.einsum('bqhd,bsd->bqhs', iqi, ik).astype(jnp.float32))
        score = jnp.einsum('bqh,bqhs->bqs', iwi, rel)
        score = jnp.where(jnp.arange(S)[None, :] <= t[:, None], score, -jnp.inf)
        _, sel = lax.top_k(score, topk)
        kg = kh[bidx, sel]
        vg = vh[bidx, sel]
        s = jnp.einsum('bqhd,bqkhd->bhqk', qi, kg).astype(jnp.float32) * (D ** -0.5)
        s = jnp.where((sel <= t[:, None])[:, None], s, -jnp.inf)
        p = jax.nn.softmax(s, axis=-1).astype(v.dtype)
        return jnp.einsum('bhqk,bqkhd->bqhd', p, vg)

    out = lax.map(chunk, (qh, iqc, iwc, jnp.arange(NQ)))
    return out.transpose(1, 0, 2, 3, 4).reshape(B, S, H * D)

def sqrelu_mlp(h, w1, w2):
    return jnp.square(jax.nn.relu(h @ w1)) @ w2

def setup_inputs(seed: int = 0) -> dict:
    key = jax.random.key(seed)
    ks = jax.random.split(key, 14)
    f32 = jnp.float32
    gain = lambda kk, shape: 1.0 + 0.05 * jax.random.normal(kk, shape, f32)
    return {
        'x': jax.random.normal(ks[0], (BATCH, SEQ, D_MODEL), f32),
        'norm_mix_pre': gain(ks[1], (DEPTH, D_MODEL)),
        'w_in': jax.random.normal(ks[2], (DEPTH, D_MODEL, D_IN), f32) * D_MODEL ** -0.5,
        'ml_conv': jax.random.normal(ks[3], (DEPTH, ML_CONV, 2 * ML_QK_W), f32) * ML_CONV ** -0.5,
        'ml_i_bias': 0.1 * jax.random.normal(ks[4], (DEPTH, ML_HEADS), f32),
        'ml_f_bias': 3.0 + 3.0 * jax.random.uniform(ks[5], (DEPTH, ML_HEADS), f32),
        'ml_head_norm': gain(ks[6], (DEPTH, ML_V_W)),
        'w_out': jax.random.normal(ks[7], (DEPTH, D_MIX, D_MODEL), f32) * D_MIX ** -0.5,
        'norm_mix_post': gain(ks[8], (DEPTH, D_MODEL)),
        'norm_mlp_pre': gain(ks[9], (DEPTH, D_MODEL)),
        'w_ff1': jax.random.normal(ks[10], (DEPTH, D_MODEL, D_FF), f32) * D_MODEL ** -0.5,
        'w_ff2': jax.random.normal(ks[11], (DEPTH, D_FF, D_MODEL), f32) * D_FF ** -0.5,
        'norm_mlp_post': gain(ks[12], (DEPTH, D_MODEL)),
    }

def reference(x, norm_mix_pre, w_in, ml_conv, ml_i_bias, ml_f_bias, ml_head_norm, w_out,
              norm_mix_post, norm_mlp_pre, w_ff1, w_ff2, norm_mlp_post):
    pts = _split_points()
    for l in range(DEPTH):
        h = rmsnorm(x, norm_mix_pre[l])
        proj = h @ w_in[l]
        (ml_q, ml_k, ml_v, ml_o, ml_i, ml_f, mb_q, mb_k, mb_v,
         ds_q, ds_k, ds_v, ix_q, ix_k, ix_w) = jnp.split(proj, pts, axis=-1)
        y_ml = mlstm_group(ml_q, ml_k, ml_v, ml_o, ml_i + ml_i_bias[l], ml_f + ml_f_bias[l],
                           ml_conv[l], ml_head_norm[l])
        y_mb = moba_group(mb_q, mb_k, mb_v)
        y_ds = dsa_group(ds_q, ds_k, ds_v, ix_q, ix_k, ix_w)
        mix = jnp.concatenate([y_ml, y_mb, y_ds], axis=-1) @ w_out[l]
        x = x + rmsnorm(mix, norm_mix_post[l])
        h = rmsnorm(x, norm_mlp_pre[l])
        x = x + rmsnorm(sqrelu_mlp(h, w_ff1[l], w_ff2[l]), norm_mlp_post[l])
    return x


_drawn_inputs = setup_inputs


def setup_inputs(seed=0):
    import zlib

    import numpy as np

    out = dict(_drawn_inputs(seed))
    spreads = {}
    factors = {'ml_i_bias': 64.0}
    for name, (base, spread) in spreads.items():
        noise = np.random.default_rng([zlib.crc32(name.encode()), seed]).standard_normal(out[name].shape)
        drawn = base * np.exp(spread * noise) if base else spread * noise
        out[name] = __import__('jax').numpy.asarray(drawn.astype(out[name].dtype))
    for name, factor in factors.items():
        out[name] = (out[name] * factor).astype(out[name].dtype)
    return out
```

```python
from contextlib import ExitStack

import concourse.bass as bass
from concourse import mybir

F32 = mybir.dt.float32
F32R = mybir.dt.float32r
ALU = mybir.AluOpType
ACT = mybir.ActivationFunctionType
AX = mybir.AxisListType

P = 128
DEPTH, SEQ, D = 2, 512, 1024
NT = SEQ // P
KD = D // P
HEADS, DK, ML_DV = 4, 64, 128
TOPK = min(256, SEQ // 4)
D_FF = 4 * D
EPS = 1e-6
W_QK, W_V, W_SM = HEADS * DK, HEADS * ML_DV, HEADS * DK
(C_MLQ, C_MLK, C_MLV, C_MLO, C_I, C_F, C_MBQ, C_MBK, C_MBV, C_DSQ, C_DSK, C_DSV, C_IXQ, C_IXK, C_IXW) = (
    0, 256, 512, 1024, 1536, 1540, 1544, 1800, 2056, 2312, 2568, 2824, 3080, 3336, 3400)

UNIT = 2048
UNITS = [("f", C_IXQ), ("f", C_MLQ), ("small", None), ("f", C_MLK), ("t", C_MLV), ("t", C_MLV + 256),
         ("f", C_MBQ), ("f", C_MBK), ("t", C_MBV), ("f", C_DSQ), ("f", C_DSK), ("t", C_DSV),
         ("t", C_MLO), ("t", C_MLO + 256)]
N_PROJ = len(UNITS)
N_OUT = 4
N_PRE = N_PROJ + N_OUT
GROUPS = 4
HID = D_FF // GROUPS // P
GU = 8

PARTS = 6
IDX_FROM = 4
HEAD_FROM = 6
N_IDX = (NT - 1) * HEADS
N_ML = NT * HEADS
N_SM = 2 * NT * HEADS
N_TASKS = N_ML + N_SM
assert (HEAD_FROM - IDX_FROM) * PARTS == N_IDX and (N_PROJ - HEAD_FROM) * PARTS == N_TASKS

MASKED = -1e30
ABSENT, TAKEN = -2e38, -3e38
SCORE_AT = {1: 0, 2: 256, 3: 640}

NORMS = ([(0, i) for i in range(NT)]
         + [(1, 0), (1, 1), (2, 0), (1, 2), (2, 1), (1, 3), (2, 2), (2, 3)]
         + [(3, i) for i in range(NT)])
NORM_AT = {k: n + 1 for n, k in enumerate(NORMS)}


def tiles_of(j):
    return 2 if j < N_PROJ and UNITS[j][0] != "t" else 4


def tiles_before(j):
    return sum(tiles_of(i) for i in range(j))


def tiles_in_part(j, part):
    n = tiles_of(j)
    return range(part * n // PARTS, (part + 1) * n // PARTS)


def events_before(j):
    return sum(tiles_of(i) for i in range(j))


GROUP_EVENTS = 4 * 2 + 4 * 4
EV_MLP = events_before(N_PRE)


def mlp_event(g, jj, t):
    before = 2 * jj if jj < 4 else 8 + 4 * (jj - 4)
    return g * GROUP_EVENTS + (EV_MLP + before + t + 1)


def dmas_of(j):
    return 5 if j < N_PROJ and UNITS[j][0] == "small" else 1

def raw_landed(j):
    return 16 * sum(dmas_of(i) for i in range(j % 2, j + 1, 2))


RAW_PRE = [raw_landed(N_PRE - 2), raw_landed(N_PRE - 1)]


def trunk(nc, x, norm_mix_pre, w_in, ml_conv, ml_i_bias, ml_f_bias, ml_head_norm, w_out,
          norm_mix_post, norm_mlp_pre, w_ff1, w_ff2, norm_mlp_post, out):
    ctx = ExitStack()
    with ctx:
        def sb(name, shape, dt=F32, on=ctx):
            return on.enter_context(nc.sbuf_tensor(name, shape, dt))

        X = sb("X", [P, NT, D])
        Y = sb("Y", [P, NT, D])
        gain_pre = sb("gain_pre", [P, D])
        gain_post = sb("gain_post", [P, D])
        head_gain = sb("head_gain", [P, W_V])
        raw = sb("raw", [P, 2, UNIT])
        w_hi = sb("w_hi", [P, 2, UNIT], F32R)
        w_lo = sb("w_lo", [P, 2, UNIT], F32R)
        hT_hi = sb("hT_hi", [P, KD, SEQ], F32R)
        hT_lo = sb("hT_lo", [P, KD, SEQ], F32R)
        sbuf_s = sb("scores", [P, 2, SEQ])
        sbuf_p = sb("probs", [P, 2, SEQ])
        sbuf_pt = sb("probs_t", [P, 2, SEQ])
        sq = sb("squares", [P, 2 * ML_DV])
        with ExitStack() as shared:
            hid_hi = sb("hid_hi", [P, HID, SEQ], F32R, shared)
            hid_lo = sb("hid_lo", [P, HID, SEQ], F32R, shared)
            hid_r = sb("hid_r", [P, 2, SEQ], on=shared)
            hid_h = sb("hid_h", [P, 2, SEQ], on=shared)
        ml_qk = sb("ml_qk", [P, 4, SEQ])
        sm_qk = [sb("mb_qk", [P, 4, SEQ]), sb("ds_qk", [P, 4, SEQ])]
        ix_q = sb("ix_q", [P, 2, SEQ])
        ix_k = sb("ix_k", [P, SEQ])
        ml_gate = sb("ml_gate", [P, NT, W_V])
        sb("pad_m", [P, (2 * HID + 4) * SEQ - 15 * SEQ - NT * W_V])
        rows_t = sb("rows_t", [P, SEQ])
        ml_v = sb("ml_v", [P, NT, HEADS, ML_DV + 1])
        sm_v = sb("sm_v", [P, NT, 2 * HEADS, DK])
        score = sb("score", [P, 1152])
        causal = sb("causal", [P, SEQ])
        ones = sb("ones", [HEADS, SEQ])
        ident = sb("ident", [P, P])
        pick = sb("pick", [HEADS, HEADS, P])
        half = sb("half", [P, HEADS])
        conv_rows = sb("conv_rows", [16, P])
        conv_w = sb("conv_w", [P, 16])
        gate_bias = sb("gate_bias", [P, 1])
        a_col = sb("a_col", [P, NT, HEADS])
        expm = sb("expm", [P, NT, HEADS])
        iw_col = sb("iw_col", [P, NT, HEADS])
        ms = sb("ms", [P, 16])
        ms_eps = sb("ms_eps", [P, 16])
        rstd = sb("rstd", [P, 16])
        hms = sb("hms", [P, NT, HEADS])
        hms_eps = sb("hms_eps", [P, NT, HEADS])
        hrstd = sb("hrstd", [P, NT, HEADS])
        den = sb("den", [P, NT, HEADS])
        rden = sb("rden", [P, NT, HEADS])
        top8 = sb("top8", [P, 8])
        nmin = sb("nmin", [P, 2])
        sums = sb("sums", [P, 2, HEADS])
        rsum = sb("rsum", [P, 2, HEADS])
        sq_sink = sb("sq_sink", [P, D], mybir.dt.bfloat16)
        rows = sbuf_pt[:, 0, :]
        relu_s = sbuf_p
        conv_in = Y[:, 0, :].rearrange("p (b t) -> p b t", b=2)
        conv_acc = Y[:, 1, :].rearrange("p (b t) -> p b t", b=2)
        g_f, g_n = Y[0:HEADS, 2, 0:SEQ], Y[0:HEADS, 2, SEQ:2 * SEQ]
        g_B, g_M = Y[0:HEADS, 3, 0:SEQ], Y[0:HEADS, 3, SEQ:2 * SEQ]

        ps = ctx.enter_context(nc.psum_tensor("ps", [P, 8, 512], F32))

        sems = []

        def sem(name, cleared=True):
            s = ctx.enter_context(nc.semaphore(name))
            if cleared:
                sems.append(s.num)
            return s

        layer_go = sem("layer_go", False)
        x_loaded = sem("x_loaded", False)
        stored = sem("stored", False)
        const_step = sem("const_step", False)
        layer_begun = sem("layer_begun", False)
        layer_end = sem("layer_end")
        params_loaded = sem("params_loaded")
        gain_pre_loaded, gain_post_loaded = sem("gain_pre_loaded"), sem("gain_post_loaded")
        raw_loaded = [sem("raw0_loaded"), sem("raw1_loaded")]
        hi_ready, lo_ready = sem("hi_ready"), sem("lo_ready")
        mm_done = sem("mm_done")
        ms_done, eps_done, rstd_done = sem("ms_done"), sem("eps_done"), sem("rstd_done")
        xn_done = sem("xn_done")
        nt_done, nhi_done, nlo_done = sem("nt_done"), sem("nhi_done"), sem("nlo_done")
        applied_t, applied = sem("applied_t"), sem("applied")
        conv_t, conv_w_ready = sem("conv_t"), sem("conv_w_ready")
        tile_out = sem("tile_out")
        conv_step, silu_done = sem("conv_step"), sem("silu_done")
        gate_step, softplus_done = sem("gate_step"), sem("softplus_done")
        iw_scaled = sem("iw_scaled")
        rows_turned, cols_done = sem("rows_turned"), sem("cols_done")
        idx_done, idx_relu, idx_acc, score_ready = sem("idx_done"), sem("idx_relu"), sem("idx_acc"), sem("score_ready")
        tk = sem("topk_step")
        spread_done, st_done, decay_done, decay_cut = sem("spread_done"), sem("st_done"), sem("decay_done"), sem("decay_cut")
        ml_p, ml_pv, ml_step, ml_fin = sem("ml_p"), sem("ml_pv"), sem("ml_step"), sem("ml_fin")
        hms_done, hms_eps_done, hrstd_done, ml_gained, ml_out = (
            sem("hms_done"), sem("hms_eps_done"), sem("hrstd_done"), sem("ml_gained"), sem("ml_out"))
        sc_done, sm_masked, exp_done, pt_done, pt_out, pv_done = (
            sem("sc_done"), sem("sm_masked"), sem("exp_done"), sem("pt_done"), sem("pt_out"), sem("pv_done"))
        rsum_done, sm_fin = sem("rsum_done"), sem("sm_fin")
        hid_relu, hid_sq, hid_hi_done, hid_ready = sem("hid_relu"), sem("hid_sq"), sem("hid_hi_done"), sem("hid_ready")
        y_zero, y_out = sem("y_zero"), sem("y_out")

        assert sems == list(range(sems[0], sems[-1] + 1))

        SLOTW = {"in": (8, 256), "t": (4, 512), "out": (2, 1024)}

        def slot(t, j, form):
            k, n = SLOTW[form]
            return t[:, j % 2, :].rearrange("p (k n) -> p k n", k=k)

        def mask_of(grp, j):
            n = (j + 1) * P
            if grp == 0 or j == 0:
                return causal[:, SEQ - n:SEQ]
            return score[:, SCORE_AT[j]:SCORE_AT[j] + n]

        def begin_layer(eng, l):
            eng.wait_ge(layer_go, l + 1)
            eng.sem_inc(layer_begun, 1)
            eng.wait_ge(x_loaded, 16)

        block = ctx.enter_context(nc.Block())

        @block.sync
        def _(sp):
            sp.dma_start(X[:], x[0].rearrange("(t p) d -> p t d", p=P)).then_inc(x_loaded, 16)

            with sp.Fori(0, DEPTH) as l:
                begin_layer(sp, l)

                def load(dst, src, s):
                    sp.dma_start(dst, src).then_inc(s, 16)

                def load_unit(j):
                    s = raw_loaded[j % 2]
                    if j >= 2:
                        sp.wait_ge(lo_ready, j - 1)
                    if j >= N_PROJ:
                        r = (j - N_PROJ) * 2 * P
                        load(slot(raw, j, "out"), w_out[l, r:r + 2 * P, :].rearrange("(k p) n -> p k n", p=P), s)
                        return
                    w = w_in[l].rearrange("(k p) n -> p k n", p=P)
                    u = UNITS[j]
                    if u[0] != "small":
                        load(slot(raw, j, "in"), w[:, :, u[1]:u[1] + 256], s)
                    else:
                        d = slot(raw, j, "in")
                        for at, c, n in ((0, C_IXK, DK), (DK, C_IXK, DK), (P, C_I, HEADS), (P + 32, C_F, HEADS),
                                         (P + 64, C_IXW, HEADS)):
                            load(d[:, :, at:at + n], w[:, :, c:c + n], s)

                load(gain_pre[:], norm_mix_pre[l][None, :].to_broadcast([P, D]), gain_pre_loaded)
                load_unit(0)
                load_unit(1)
                load(conv_rows[:], ml_conv[l].rearrange("k (c p) -> (k c) p", p=P), params_loaded)
                load(gate_bias[0:HEADS, :], ml_i_bias[l][:, None], params_loaded)
                load(gate_bias[32:32 + HEADS, :], ml_f_bias[l][:, None], params_loaded)
                load(head_gain[:], ml_head_norm[l][None, :].to_broadcast([P, W_V]), params_loaded)
                load(gain_post[:], norm_mix_post[l][None, :].to_broadcast([P, D]), gain_post_loaded)
                for j in range(2, N_PRE):
                    load_unit(j)
                    if j == 4:
                        sp.wait_ge(xn_done, NT)
                        load(gain_pre[:], norm_mlp_pre[l][None, :].to_broadcast([P, D]), gain_pre_loaded)
                with sp.Fori(0, GROUPS) as g:
                    for jj in range(GU):
                        sp.wait_ge(lo_ready, g * GU + (N_PRE + jj - 1))
                        sp.wait_ge(x_loaded, 16)
                        if jj < 4:
                            src = w_ff1[l].rearrange("(k p) n -> p k n", p=P)[
                                :, :, bass.ds(g * (HID * P) + jj * 256, 256)]
                            load(slot(raw, jj, "in"), src, raw_loaded[jj % 2])
                        else:
                            c, half_k = (jj - 4) // 2, jj % 2
                            src = w_ff2[l, bass.ds(g * (HID * P) + half_k * 4 * P, 4 * P), c * 512:(c + 1) * 512]
                            load(slot(raw, jj, "t"), src.rearrange("(k p) n -> p k n", p=P), raw_loaded[jj % 2])
                sp.wait_ge(applied, NT)
                load(gain_post[:], norm_mlp_post[l][None, :].to_broadcast([P, D]), gain_post_loaded)
                sp.wait_ge(gain_post_loaded, 32)
                sp.sem_inc(layer_end, 1)
            sp.wait_ge(layer_go, DEPTH + 1)
            sp.dma_start(out[0].rearrange("(t p) d -> p t d", p=P), X[:]).then_inc(stored, 16)
            sp.wait_ge(stored, 16)

        def head_pair(pool, p):
            j, a = p // 2, 2 * (p % 2)
            y = Y[:, j, a * ML_DV:(a + 2) * ML_DV]
            pool.wait_ge(hms_done, p + 1)
            nc.gpsimd.tensor_scalar(hms_eps[:, j, a:a + 2], hms[:, j, a:a + 2], 1.0 / ML_DV, EPS, ALU.mult,
                                    ALU.add).then_inc(hms_eps_done, 1)
            nc.gpsimd.tensor_tensor(y, y, head_gain[:, a * ML_DV:(a + 2) * ML_DV], ALU.mult).then_inc(ml_gained, 1)
            pool.wait_ge(hms_eps_done, p + 1)
            nc.gpsimd.tensor_tensor(hrstd[:, j, a:a + 2], hms_eps[:, j, a:a + 2], half[:, 0:2],
                                    ALU.pow).then_inc(hrstd_done, 1)

        @block.gpsimd
        def _(pool):
            steps = [0]

            def step(ins):
                steps[0] += 1
                ins.then_inc(const_step, 1)
                pool.wait_ge(const_step, steps[0])

            step(pool.memset(ident[:], 0.0))
            step(pool.affine_select(out=ident[:], in_=ident[:], compare_op=ALU.not_equal, fill=1.0, base=0,
                                    pattern=[[-1, P]], channel_multiplier=1))
            step(pool.memset(pick[:], 1.0))
            step(pool.affine_select(out=pick[:], in_=pick[:], compare_op=ALU.is_equal, fill=0.0, base=0,
                                    pattern=[[-1, HEADS], [0, P]], channel_multiplier=1))
            step(pool.memset(causal[:], 0.0))
            step(pool.affine_select(out=causal[:, SEQ - P:SEQ], in_=causal[:, SEQ - P:SEQ], compare_op=ALU.is_ge,
                                    fill=MASKED, base=0, pattern=[[-1, P]], channel_multiplier=1))
            step(pool.memset(half[:], -0.5))
            step(pool.memset(ones[:], 1.0))
            step(pool.memset(rows_t[:], 0.0))
            step(pool.memset(ml_v[:], 1.0))
            pool.sem_inc(layer_go, 1)

            with pool.Fori(0, DEPTH) as l:
                def make_rstd(norm, i):
                    n = NORM_AT[norm, i]
                    c = slice(n - 1, n)
                    pool.wait_ge(ms_done, n)
                    nc.gpsimd.tensor_scalar(ms_eps[:, c], ms[:, c], EPS, None, ALU.add).then_inc(eps_done, 1)
                    pool.wait_ge(eps_done, n)
                    nc.gpsimd.tensor_tensor(rstd[:, c], ms_eps[:, c], half[:, 0:1], ALU.pow).then_inc(rstd_done, 1)

                for norm, i in NORMS[:NT]:
                    make_rstd(norm, i)
                for j in range(1, NT):
                    pool.wait_ge(idx_acc, HEADS * j)
                    d = score[:, SCORE_AT[j] + j * P:SCORE_AT[j] + (j + 1) * P]
                    nc.gpsimd.affine_select(out=d, in_=d, compare_op=ALU.is_ge, fill=ABSENT, base=0,
                                            pattern=[[-1, P]], channel_multiplier=1).then_inc(score_ready, 1)
                pool.wait_ge(params_loaded, 64)
                for n in range(N_ML):
                    j = n // HEADS
                    pool.wait_ge(decay_done, n + 1)
                    d = sbuf_s[:, n % 2, j * P:(j + 1) * P]
                    nc.gpsimd.affine_select(out=d, in_=d, compare_op=ALU.is_ge, fill=0.0, base=0,
                                            pattern=[[1, P]], channel_multiplier=-1).then_inc(decay_cut, 1)
                    if n >= 5 and n % 2:
                        head_pair(pool, (n - 5) // 2)
                for p in range(N_ML // 2 - 2, N_ML // 2):
                    head_pair(pool, p)
                for norm, i in NORMS[NT:]:
                    make_rstd(norm, i)
                pool.wait_ge(rstd_done, len(NORMS))
                pool.wait_ge(layer_end, 4)
                pool.sem_clear(range(sems[0], sems[-1] + 1))
                pool.sem_inc(layer_go, 1)

        @block.scalar
        def _(act):
            with act.Fori(0, DEPTH) as l:
                begin_layer(act, l)
                norm_count = [0]

                def mean_square(norm, i, src):
                    n = NORM_AT[norm, i]
                    if n >= 2:
                        act.wait_ge(ms_done, n - 1)
                    nc.scalar.activation(sq_sink[:], src, ACT.Square, scale=D ** -0.5,
                                         accum_out=ms[:, n - 1:n]).then_inc(ms_done, 1)

                def split_hi(j):
                    act.wait_ge(raw_loaded[j % 2], raw_landed(j))
                    if j >= 2:
                        act.wait_ge(mm_done, events_before(j - 1))
                    nc.scalar.copy(w_hi[:, j % 2], raw[:, j % 2]).then_inc(hi_ready, 1)

                def split_hi_mlp(g, jj):
                    act.wait_ge(raw_loaded[jj % 2], g * 64 + (RAW_PRE[jj % 2] + 16 * (jj // 2 + 1)))
                    act.wait_ge(mm_done, unit_end(g, jj - 2))
                    nc.scalar.copy(w_hi[:, jj % 2], raw[:, jj % 2]).then_inc(hi_ready, 1)

                def norm_hi(stage, i):
                    for c in range(2):
                        n = 8 * stage + 2 * i + c + 1
                        act.wait_ge(nt_done, n)
                        nc.scalar.copy(hT_hi[:, 4 * c:4 * c + 4, i * P:(i + 1) * P],
                                       ps[:, 2 * i + c, :].rearrange("p (k t) -> p k t", k=4)).then_inc(nhi_done, 1)

                for i in range(NT):
                    mean_square(0, i, X[:, i])
                split_hi(0)
                for i in range(NT):
                    norm_hi(0, i)
                split_hi(1)

                def index_relu(n):
                    j, h = n // HEADS + 1, n % HEADS
                    act.wait_ge(idx_done, n + 1)
                    if n >= 2:
                        act.wait_ge(idx_acc, n - 1)
                    nc.scalar.activation(relu_s[:, n % 2, :(j + 1) * P], ps[:, 2 + n % 2, :(j + 1) * P],
                                         ACT.Relu).then_inc(idx_relu, 1)

                def tile_copy(j, t):
                    kind, col = UNITS[j]
                    x = tiles_before(j) + t
                    act.wait_ge(mm_done, x + 1)
                    if kind == "t":
                        src = ps[:, x % 2, 0:256]
                        if col in (C_MLV, C_MLV + 256):
                            h = (col - C_MLV) // ML_DV
                            ins = nc.scalar.copy(ml_v[:, t, h:h + 2, 0:ML_DV], src.rearrange("p (h e) -> p h e", h=2))
                        elif col in (C_MLO, C_MLO + 256):
                            ins = nc.scalar.activation(ml_gate[:, t, col - C_MLO:col - C_MLO + 256], src, ACT.Sigmoid)
                        else:
                            h = HEADS * (col == C_DSV)
                            ins = nc.scalar.copy(sm_v[:, t, h:h + HEADS], src.rearrange("p (h e) -> p h e", h=HEADS))
                    else:
                        src = ps[:, x % 2, :]
                        if kind == "small":
                            ins = (nc.scalar.copy(ix_k[:], src) if t == 0 else
                                   nc.scalar.copy(rows[0:68, :], src[0:68, :]))
                        elif col in (C_MLQ, C_MLK):
                            chunk = t + 2 * (col == C_MLK)
                            if chunk >= 2:
                                act.wait_ge(conv_step, 4 * (chunk - 1))
                            ins = nc.scalar.copy(conv_in[:, chunk % 2], src)
                        else:
                            dst, at = {C_IXQ: (ix_q, 0), C_MBQ: (sm_qk[0], 0), C_MBK: (sm_qk[0], 2),
                                       C_DSQ: (sm_qk[1], 0), C_DSK: (sm_qk[1], 2)}[col]
                            ins = nc.scalar.copy(dst[:, at + t], src)
                    ins.then_inc(tile_out, 1)

                def decay(n):
                    j, h = divmod(n, HEADS)
                    if h == 0:
                        act.wait_ge(spread_done, j + 1)
                        act.wait_ge(cols_done, 3)
                    if n >= 2:
                        act.wait_ge(ml_p, n - 1)
                    for i in range(j + 1):
                        ins = nc.scalar.activation(sbuf_s[:, n % 2, i * P:(i + 1) * P],
                                                   ps[:, 4 + j % 2, h * P:(h + 1) * P], ACT.Exp,
                                                   bias=a_col[:, i, h:h + 1], scale=-1.0)
                    ins.then_inc(decay_done, 1)

                def sm_exp(m):
                    k, h = divmod(m, HEADS)
                    w = (k % NT + 1) * P
                    act.wait_ge(sm_masked, m + 1)
                    if m >= 2:
                        act.wait_ge(pt_done, m - 1)
                    if h == 0 and k >= 2:
                        act.wait_ge(rsum_done, k - 1)
                    nc.scalar.activation(sbuf_p[:, m % 2, :w], sbuf_s[:, m % 2, :w], ACT.Exp,
                                         bias=nmin[:, m % 2:m % 2 + 1], scale=-1.0,
                                         accum_out=sums[:, k % 2, h:h + 1]).then_inc(exp_done, 1)

                def pt_copy(m):
                    w = (m // HEADS % NT + 1) * P
                    act.wait_ge(pt_done, m + 1)
                    if m >= 2:
                        act.wait_ge(pv_done, m - 1)
                    nc.scalar.copy(sbuf_pt[:, m % 2, :w], ps[:, 4 + m % 2, :w]).then_inc(pt_out, 1)

                def head_step(n):
                    if n < N_ML:
                        decay(n)
                    elif n < N_TASKS:
                        sm_exp(n - N_ML)
                    if n > N_ML:
                        pt_copy(n - 1 - N_ML)

                for j in range(IDX_FROM):
                    for t in range(tiles_of(j)):
                        tile_copy(j, t)
                    split_hi(j + 2)
                    if j in (1, 3):
                        for chunk in (j - 1, j):
                            act.wait_ge(conv_step, 4 * (chunk + 1))
                            nc.scalar.activation(ml_qk[:, chunk], conv_acc[:, chunk % 2], ACT.Silu).then_inc(silu_done, 1)
                    if j == 2:
                        act.wait_ge(tile_out, 6)
                        nc.scalar.mul(rows_t[64:64 + HEADS, :], rows[64:64 + HEADS, :],
                                      (HEADS * DK) ** -0.5).then_inc(iw_scaled, 1)
                        act.wait_ge(gate_step, 2)
                        nc.scalar.activation(g_n, g_n, ACT.Exp).then_inc(softplus_done, 1)
                        act.wait_ge(softplus_done, 1)
                        nc.scalar.activation(g_n, g_n, ACT.Ln, bias=1.0).then_inc(softplus_done, 1)
                act.wait_ge(rows_turned, 1)
                r = ps[:, 4, 0:NT * 68].rearrange("p (t c) -> p t c", t=NT)
                nc.scalar.copy(a_col[:], r[:, :, 0:HEADS]).then_inc(cols_done, 1)
                nc.scalar.copy(iw_col[:], r[:, :, 64:64 + HEADS]).then_inc(cols_done, 1)
                nc.scalar.activation(expm[:], r[:, :, 32:32 + HEADS], ACT.Exp, scale=-1.0).then_inc(cols_done, 1)

                for j in range(IDX_FROM, N_PROJ):
                    for part in range(PARTS):
                        for t in tiles_in_part(j, part):
                            tile_copy(j, t)
                        if part == PARTS - 1:
                            split_hi(j + 2)
                        if j < HEAD_FROM:
                            index_relu((j - IDX_FROM) * PARTS + part)
                        else:
                            head_step((j - HEAD_FROM) * PARTS + part)
                head_step(N_TASKS)

                for n in range(2 * NT):
                    c, i = divmod(n, NT)
                    act.wait_ge(nt_done, 8 + n + 1)
                    nc.scalar.copy(hT_hi[:, 4 * c:4 * c + 4, i * P:(i + 1) * P],
                                   ps[:, n, :].rearrange("p (k t) -> p k t", k=4)).then_inc(nhi_done, 1)
                split_hi(N_PROJ + 2)
                split_hi(N_PROJ + 3)
                act.wait_ge(raw_loaded[0], RAW_PRE[0] + 16)
                act.wait_ge(mm_done, events_before(N_PRE - 1))
                nc.scalar.copy(w_hi[:, 0], raw[:, 0]).then_inc(hi_ready, 1)

                last = events_before(N_PRE - 1)

                def mix_square(i):
                    act.wait_ge(mm_done, last + i + 1)
                    mean_square(1, i, ps[:, 2 * i:2 * i + 2, :].rearrange("p a b -> p (a b)"))

                def x_square(i):
                    act.wait_ge(applied, i + 1)
                    mean_square(2, i, X[:, i])

                mix_square(0)
                mix_square(1)
                x_square(0)
                mix_square(2)
                x_square(1)
                norm_hi(2, 0)
                mix_square(3)
                x_square(2)
                norm_hi(2, 1)
                x_square(3)
                norm_hi(2, 2)
                norm_hi(2, 3)
                split_hi_mlp(0, 1)

                def hidden(g, m):
                    act.wait_ge(mm_done, mlp_event(g, m // 2, m % 2))
                    act.wait_ge(hid_ready, g * HID + m + 1)
                    nc.scalar.activation(hid_r[:, m % 2], ps[:, m, :], ACT.Relu).then_inc(hid_relu, 1)
                    act.wait_ge(hid_relu, g * HID + m + 1)
                    nc.scalar.activation(hid_hi[:, m], hid_r[:, m % 2], ACT.Square).then_inc(hid_hi_done, 1)

                def group(g, is_last):
                    for jj in range(GU):
                        if jj < 4:
                            hidden(g, 2 * jj)
                            hidden(g, 2 * jj + 1)
                        if jj + 2 < GU:
                            split_hi_mlp(g, jj + 2)
                        elif not is_last:
                            split_hi_mlp(g + 1, jj + 2 - GU)

                with act.Fori(0, GROUPS - 1) as g:
                    group(g, False)
                group(GROUPS - 1, True)
                for i in range(NT):
                    act.wait_ge(y_out, 8 * GROUPS + 8 + i - 3)
                    mean_square(3, i, Y[:, i])
                act.wait_ge(ms_done, len(NORMS))
                act.sem_inc(layer_end, 1)

        @block.vector
        def _(dve):
            with dve.Fori(0, DEPTH) as l:
                begin_layer(dve, l)

                def split_lo(n, j):
                    dve.wait_ge(hi_ready, n + 1)
                    nc.vector.tensor_tensor(w_lo[:, j % 2], raw[:, j % 2], w_hi[:, j % 2].bitcast(F32),
                                            ALU.subtract).then_inc(lo_ready, 1)

                def normed(norm, i):
                    dve.wait_ge(rstd_done, NORM_AT[norm, i])
                    dve.wait_ge(gain_pre_loaded, 16 if norm == 0 else 32)
                    c = NORM_AT[norm, i] - 1
                    nc.vector.scalar_tensor_tensor(Y[:, i], X[:, i], rstd[:, c:c + 1], gain_pre[:], ALU.mult,
                                                   ALU.mult).then_inc(xn_done, 1)

                def norm_lo(stage, i):
                    for c in range(2):
                        n = 8 * stage + 2 * i + c + 1
                        dve.wait_ge(nhi_done, n)
                        nc.vector.tensor_tensor(
                            hT_lo[:, 4 * c:4 * c + 4, i * P:(i + 1) * P],
                            ps[:, 2 * i + c, :].rearrange("p (k t) -> p k t", k=4),
                            hT_hi[:, 4 * c:4 * c + 4, i * P:(i + 1) * P].bitcast(F32), ALU.subtract).then_inc(nlo_done, 1)

                def apply(norm, i, src):
                    n = i + 1 + (NT if norm == 3 else 0)
                    c = NORM_AT[norm, i] - 1
                    dve.wait_ge(rstd_done, c + 1)
                    dve.wait_ge(gain_post_loaded, 16 if norm == 1 else 32)
                    nc.vector.scalar_tensor_tensor(Y[:, i], src, rstd[:, c:c + 1], gain_post[:], ALU.mult,
                                                   ALU.mult).then_inc(applied_t, 1)
                    dve.wait_ge(applied_t, n)
                    nc.vector.tensor_tensor(X[:, i], X[:, i], Y[:, i], ALU.add).then_inc(applied, 1)

                for i in range(NT):
                    normed(0, i)
                split_lo(0, 0)
                for i in range(NT):
                    norm_lo(0, i)
                split_lo(1, 1)

                def conv(chunk):
                    acc, src = conv_acc[:, chunk % 2], conv_in[:, chunk % 2]
                    dve.wait_ge(tile_out, 3 + chunk + 2 * (chunk >= 2))
                    dve.wait_ge(conv_w_ready, 1)
                    if chunk >= 2:
                        dve.wait_ge(silu_done, chunk - 1)
                    for n, k in enumerate((3, 2, 1, 0)):
                        w = conv_w[:, 4 * k + chunk:4 * k + chunk + 1]
                        d = 3 - k
                        if n == 0:
                            ins = nc.vector.tensor_scalar(acc, src, w, None, ALU.mult)
                        else:
                            dve.wait_ge(conv_step, 4 * chunk + n)
                            ins = nc.vector.scalar_tensor_tensor(acc[:, d:], src[:, :SEQ - d], w, acc[:, d:],
                                                                 ALU.mult, ALU.add)
                        ins.then_inc(conv_step, 1)

                def gates_f():
                    dve.wait_ge(params_loaded, 64)
                    dve.wait_ge(tile_out, 6)
                    nc.vector.tensor_scalar(g_f, rows[32:32 + HEADS, :], gate_bias[32:32 + HEADS, :], None,
                                            ALU.add).then_inc(gate_step, 1)
                    dve.wait_ge(gate_step, 1)
                    nc.vector.scalar_tensor_tensor(g_n, g_f, -1.0, g_f, ALU.mult, ALU.min).then_inc(gate_step, 1)

                def gates_scan():
                    dve.wait_ge(softplus_done, 2)
                    nc.vector.scalar_tensor_tensor(g_f, g_f, 0.0, g_n, ALU.min, ALU.subtract).then_inc(gate_step, 1)
                    dve.wait_ge(gate_step, 3)
                    nc.vector.tensor_tensor_scan(g_B, ones[:], g_f, 0.0, ALU.mult, ALU.add).then_inc(gate_step, 1)
                    dve.wait_ge(gate_step, 4)
                    nc.vector.scalar_tensor_tensor(rows_t[0:HEADS, :], rows[0:HEADS, :], gate_bias[0:HEADS, :], g_B,
                                                   ALU.add, ALU.subtract).then_inc(gate_step, 1)
                    dve.wait_ge(gate_step, 5)
                    nc.vector.tensor_tensor_scan(g_M, rows_t[0:HEADS, :], rows_t[0:HEADS, :], 0.0, ALU.max,
                                                 ALU.max).then_inc(gate_step, 1)
                    dve.wait_ge(gate_step, 6)
                    nc.vector.tensor_tensor(rows_t[32:32 + HEADS, :], g_B, g_M, ALU.add).then_inc(gate_step, 1)

                def index_sum(n):
                    j, h = n // HEADS + 1, n % HEADS
                    w = (j + 1) * P
                    acc = score[:, SCORE_AT[j]:SCORE_AT[j] + w]
                    dve.wait_ge(idx_relu, n + 1)
                    if h == 0:
                        dve.wait_ge(cols_done, 2)
                        ins = nc.vector.tensor_scalar(acc, relu_s[:, n % 2, :w], iw_col[:, j, h:h + 1], None, ALU.mult)
                    else:
                        dve.wait_ge(idx_acc, n)
                        ins = nc.vector.scalar_tensor_tensor(acc, relu_s[:, n % 2, :w], iw_col[:, j, h:h + 1], acc,
                                                             ALU.mult, ALU.add)
                    ins.then_inc(idx_acc, 1)

                ROUNDS = TOPK // 8
                STEPS = 2 * ROUNDS + 2

                def topk(r):
                    j, r = divmod(r, ROUNDS)
                    j += 1
                    sc = score[:, SCORE_AT[j]:SCORE_AT[j] + (j + 1) * P]
                    at = STEPS * (j - 1) + 2 * r
                    if r == 0:
                        dve.wait_ge(score_ready, j)
                    if at:
                        dve.wait_ge(tk, at)
                    nc.vector.max(top8[:], sc).then_inc(tk, 1)
                    dve.wait_ge(tk, at + 1)
                    nc.vector.match_replace(sc, top8[:], sc, TAKEN).then_inc(tk, 1)
                    if r == ROUNDS - 1:
                        dve.wait_ge(tk, at + 2)
                        nc.vector.tensor_scalar(sc, sc, TAKEN, None, ALU.is_equal).then_inc(tk, 1)
                        dve.wait_ge(tk, at + 3)
                        nc.vector.tensor_scalar(sc, sc, -MASKED, MASKED, ALU.mult, ALU.add).then_inc(tk, 1)

                def ml_probs(n):
                    w = (n // HEADS + 1) * P
                    dve.wait_ge(st_done, n + 1)
                    dve.wait_ge(decay_cut, n + 1)
                    if n >= 2:
                        dve.wait_ge(ml_pv, n - 1)
                    nc.vector.scalar_tensor_tensor(sbuf_pt[:, n % 2, :w], ps[:, 2 + n % 2, :w], DK ** -0.5,
                                                   sbuf_s[:, n % 2, :w], ALU.mult, ALU.mult).then_inc(ml_p, 1)

                def ml_divide(p):
                    j, a = p // 2, 2 * (p % 2)
                    o = ps[:, 6 + p % 2, 0:2 * (ML_DV + 1)].rearrange("p (h e) -> p h e", h=2)
                    y = Y[:, j, a * ML_DV:(a + 2) * ML_DV].rearrange("p (h e) -> p h e", h=2)
                    d, r = den[:, j, a:a + 2], rden[:, j, a:a + 2]
                    dve.wait_ge(ml_pv, 2 * (p + 1))
                    nc.vector.scalar_tensor_tensor(d, o[:, :, ML_DV], -1.0, expm[:, j, a:a + 2], ALU.mult,
                                                   ALU.max).then_inc(ml_step, 1)
                    dve.wait_ge(ml_step, 4 * p + 1)
                    nc.vector.tensor_tensor(d, o[:, :, ML_DV], d, ALU.max).then_inc(ml_step, 1)
                    dve.wait_ge(ml_step, 4 * p + 2)
                    nc.vector.reciprocal(r, d).then_inc(ml_step, 1)
                    dve.wait_ge(ml_step, 4 * p + 3)
                    nc.vector.tensor_tensor(y, o[:, :, 0:ML_DV], r[:, :, None].to_broadcast([P, 2, ML_DV]),
                                            ALU.mult).then_inc(ml_fin, 1)
                    dve.wait_ge(ml_fin, p + 1)
                    if p:
                        dve.wait_ge(hms_done, p)
                    nc.vector.tensor_tensor(sq[:].rearrange("p (h e) -> p h e", h=2), y, y, ALU.mult).then_inc(ml_step, 1)
                    dve.wait_ge(ml_step, 4 * p + 4)
                    nc.vector.tensor_reduce(hms[:, j, a:a + 2], sq[:].rearrange("p (h e) -> p h e", h=2), AX.X,
                                            ALU.add).then_inc(hms_done, 1)

                def ml_gated(j, a):
                    dve.wait_ge(hrstd_done, 2 * j + a // 2 + 1)
                    dve.wait_ge(ml_gained, 2 * j + a // 2 + 1)
                    dve.wait_ge(tile_out, tiles_before(N_PROJ - 2 + a // 2) + j + 1)
                    for h in (a, a + 1):
                        y = Y[:, j, h * ML_DV:(h + 1) * ML_DV]
                        ins = nc.vector.scalar_tensor_tensor(y, y, hrstd[:, j, h:h + 1],
                                                             ml_gate[:, j, h * ML_DV:(h + 1) * ML_DV], ALU.mult,
                                                             ALU.mult)
                    ins.then_inc(ml_out, 1)

                def sm_mask(m):
                    grp, j = divmod(m // HEADS, NT)
                    w = (j + 1) * P
                    dve.wait_ge(sc_done, m + 1)
                    if m >= 2:
                        dve.wait_ge(exp_done, m - 1)
                    if grp == 1 and j:
                        dve.wait_ge(tk, STEPS * j)
                    nc.vector.tensor_tensor_reduce(sbuf_s[:, m % 2, :w], ps[:, 2 + m % 2, :w], mask_of(grp, j),
                                                   -DK ** -0.5, 3e38, ALU.add, ALU.min,
                                                   nmin[:, m % 2:m % 2 + 1]).then_inc(sm_masked, 1)

                def sm_divide(k):
                    grp, j = divmod(k, NT)
                    dve.wait_ge(pv_done, HEADS * (k + 1))
                    nc.vector.reciprocal(rsum[:, k % 2], sums[:, k % 2]).then_inc(rsum_done, 1)
                    dve.wait_ge(rsum_done, k + 1)
                    c = W_V + grp * W_SM
                    nc.vector.tensor_tensor(Y[:, j, c:c + W_SM].rearrange("p (h e) -> p h e", h=HEADS),
                                            ps[:, 6 + k % 2, 0:W_SM].rearrange("p (h e) -> p h e", h=HEADS),
                                            rsum[:, k % 2][:, :, None].to_broadcast([P, HEADS, DK]),
                                            ALU.mult).then_inc(sm_fin, 1)

                def head_step(n):
                    if N_ML <= n < N_TASKS:
                        sm_mask(n - N_ML)
                    if 1 <= n <= N_ML:
                        ml_probs(n - 1)
                    if n % 2 == 0 and 4 <= n <= N_ML + 2:
                        ml_divide((n - 4) // 2)
                    if n % HEADS == 2 and n >= N_ML + 6:
                        sm_divide((n - N_ML - 6) // HEADS)
                    if n < 3 * ROUNDS - PARTS:
                        topk(n + PARTS)

                for j in range(IDX_FROM):
                    if j == 0:
                        dve.wait_ge(conv_t, 1)
                        nc.vector.tensor_copy(conv_w[:], ps[:, 4, 0:16]).then_inc(conv_w_ready, 1)
                    split_lo(j + 2, j + 2)
                    if j == 1:
                        conv(0)
                        conv(1)
                    if j == 2:
                        gates_f()
                        gates_scan()
                    if j == 3:
                        conv(2)
                        conv(3)
                for j in range(IDX_FROM, N_PROJ):
                    for part in range(PARTS):
                        if part == 0 and j > IDX_FROM:
                            split_lo(j + 1, j + 1)
                        if j < HEAD_FROM:
                            index_sum((j - IDX_FROM) * PARTS + part)
                            if j == HEAD_FROM - 1:
                                topk(part)
                        else:
                            head_step((j - HEAD_FROM) * PARTS + part)
                        if j == N_PROJ - 1 and part < NT:
                            ml_gated(part, 0)
                split_lo(N_PROJ + 1, N_PROJ + 1)
                for i in range(NT):
                    ml_gated(i, 2)
                sm_divide(2 * NT - 1)

                for n in range(2 * NT):
                    c, i = divmod(n, NT)
                    dve.wait_ge(nhi_done, 8 + n + 1)
                    nc.vector.tensor_tensor(
                        hT_lo[:, 4 * c:4 * c + 4, i * P:(i + 1) * P], ps[:, n, :].rearrange("p (k t) -> p k t", k=4),
                        hT_hi[:, 4 * c:4 * c + 4, i * P:(i + 1) * P].bitcast(F32), ALU.subtract).then_inc(nlo_done, 1)
                for j in range(N_PROJ + 2, N_PRE + 1):
                    split_lo(j, j)

                def mixed(i):
                    apply(1, i, ps[:, 2 * i:2 * i + 2, :].rearrange("p a b -> p (a b)"))

                mixed(0)
                mixed(1)
                normed(2, 0)
                mixed(2)
                normed(2, 1)
                norm_lo(2, 0)
                mixed(3)
                normed(2, 2)
                norm_lo(2, 1)
                normed(2, 3)
                norm_lo(2, 2)
                norm_lo(2, 3)
                split_lo(N_PRE + 1, 1)
                dve.wait_ge(nt_done, 24)
                for i in range(NT):
                    nc.vector.memset(Y[:, i], 0.0).then_inc(y_zero, 1)
                dve.sem_inc(y_out, 8)
                dve.sem_inc(hid_ready, 2)
                dve.wait_ge(y_zero, NT)

                def hidden(g, m):
                    dve.wait_ge(hid_ready, g * HID + m + 1)
                    dve.wait_ge(hid_relu, g * HID + m + 1)
                    nc.vector.tensor_tensor(hid_h[:, m % 2], hid_r[:, m % 2], hid_r[:, m % 2],
                                            ALU.mult).then_inc(hid_sq, 1)
                    dve.wait_ge(hid_hi_done, g * HID + m + 1)
                    dve.wait_ge(hid_sq, g * HID + m + 1)
                    nc.vector.tensor_tensor(hid_lo[:, m], hid_h[:, m % 2], hid_hi[:, m].bitcast(F32),
                                            ALU.subtract).then_inc(hid_ready, 1)

                def y_add(g, c, i):
                    dve.wait_ge(mm_done, mlp_event(g, 5 + 2 * c, i))
                    dve.wait_ge(y_out, g * 8 + (4 * c + i + 1))
                    y = Y[:, i, c * 512:(c + 1) * 512]
                    nc.vector.tensor_tensor(y, y, ps[:, 4 * c + i, :], ALU.add).then_inc(y_out, 1)

                def group(g, is_last):
                    for jj in range(GU):
                        if jj < 4:
                            hidden(g, 2 * jj)
                            hidden(g, 2 * jj + 1)
                        if jj + 2 < GU or not is_last:
                            split_lo(g * GU + (N_PRE + jj + 2), jj)
                        if jj == 5 or jj == 7:
                            for i in range(NT):
                                y_add(g, (jj - 5) // 2, i)

                with dve.Fori(0, GROUPS - 1) as g:
                    group(g, False)
                group(GROUPS - 1, True)
                for i in range(NT):
                    apply(3, i, Y[:, i])
                dve.wait_ge(applied, 2 * NT)
                dve.sem_inc(layer_end, 1)

        @block.tensor
        def _(pe):
            pe.wait_ge(const_step, 10)
            with pe.Fori(0, DEPTH) as l:
                begin_layer(pe, l)

                def turn(stage, i):
                    for c in range(2):
                        for q in range(4):
                            k = 4 * c + q
                            ins = nc.tensor.transpose(ps[:, 2 * i + c, q * P:(q + 1) * P],
                                                      Y[:, i, k * P:(k + 1) * P], ident[:])
                        ins.then_inc(nt_done, 1)

                def passes(o, st, mv, first, final):
                    nc.tensor.matmul(o, st[0], mv[1], start=first, stop=False)
                    nc.tensor.matmul(o, st[0], mv[0], start=False, stop=False)
                    return nc.tensor.matmul(o, st[1], mv[0], start=False, stop=final)

                def unit_part(j, part):
                    kind = UNITS[j][0]
                    hi, lo = slot(w_hi, j, "in"), slot(w_lo, j, "in")
                    n = tiles_of(j) * KD * 3 // PARTS
                    for at in range(part * n, (part + 1) * n):
                        t, k, which = at // (3 * KD), at // 3 % KD, at % 3
                        x = tiles_before(j) + t
                        if at == 0:
                            pe.wait_ge(lo_ready, j + 1)
                        if at % (3 * KD) == 0 and x >= 2:
                            pe.wait_ge(tile_out, x - 1)
                        s = slice(t * P, (t + 1) * P)
                        first, final = at % (3 * KD) == 0, at % (3 * KD) == 3 * KD - 1
                        st_hi, st_lo = (hT_hi[:, k, s], hT_lo[:, k, s]) if kind == "t" else (hi[:, k, s], lo[:, k, s])
                        mv_hi, mv_lo = (hi[:, k, :], lo[:, k, :]) if kind == "t" else (hT_hi[:, k, :], hT_lo[:, k, :])
                        ins = nc.tensor.matmul(ps[:, x % 2, 0:256] if kind == "t" else ps[:, x % 2, :],
                                               st_lo if which == 2 else st_hi, mv_lo if which == 0 else mv_hi,
                                               start=first, stop=final)
                        if final:
                            ins.then_inc(mm_done, 1)

                for i in range(NT):
                    pe.wait_ge(xn_done, i + 1)
                    turn(0, i)

                def index_scores(n):
                    j, h = n // HEADS + 1, n % HEADS
                    if n == 0:
                        pe.wait_ge(tile_out, tiles_before(3))
                    if n >= 2:
                        pe.wait_ge(idx_relu, n - 1)
                    b = DK * (h % 2)
                    nc.tensor.matmul(ps[:, 2 + n % 2, :(j + 1) * P], ix_q[b:b + DK, h // 2, j * P:(j + 1) * P],
                                     ix_k[b:b + DK, :(j + 1) * P], start=True, stop=True).then_inc(idx_done, 1)

                def ml_spread(j):
                    if j == 0:
                        pe.wait_ge(cols_done, 3)
                    if j >= 2:
                        pe.wait_ge(decay_done, HEADS * (j - 1))
                    for h in range(HEADS):
                        ins = nc.tensor.matmul(ps[:, 4 + j % 2, h * P:(h + 1) * P], pick[:, h, :],
                                               g_M[:, j * P:(j + 1) * P], start=True, stop=True)
                    ins.then_inc(spread_done, 1)

                def ml_scores(n):
                    j, h = divmod(n, HEADS)
                    b = DK * (h % 2)
                    if n == 0:
                        pe.wait_ge(silu_done, 4)
                    if n < 2:
                        pe.wait_ge(idx_relu, N_IDX)
                    else:
                        pe.wait_ge(ml_p, n - 1)
                    for i in range(j + 1):
                        ins = nc.tensor.matmul(ps[:, 2 + n % 2, i * P:(i + 1) * P],
                                               ml_qk[b:b + DK, 2 + h // 2, i * P:(i + 1) * P],
                                               ml_qk[b:b + DK, h // 2, j * P:(j + 1) * P], start=True, stop=True)
                    ins.then_inc(st_done, 1)

                def ml_values(n):
                    j, h = divmod(n, HEADS)
                    p = n // 2
                    pe.wait_ge(ml_p, n + 1)
                    if n == 0:
                        pe.wait_ge(tile_out, tiles_before(HEAD_FROM))
                    if n % 2 == 0 and p >= 2:
                        pe.wait_ge(ml_fin, p - 1)
                    c = (ML_DV + 1) * (n % 2)
                    for i in range(j + 1):
                        ins = nc.tensor.matmul(ps[:, 6 + p % 2, c:c + ML_DV + 1],
                                               sbuf_pt[:, n % 2, i * P:(i + 1) * P], ml_v[:, i, h, :],
                                               start=(i == 0), stop=(i == j))
                    ins.then_inc(ml_pv, 1)

                def sm_scores(m):
                    k, h = divmod(m, HEADS)
                    grp, j = divmod(k, NT)
                    b = DK * (h % 2)
                    if m % N_ML == 0:
                        pe.wait_ge(tile_out, tiles_before(8 if grp == 0 else 11))
                    if m < 2:
                        pe.wait_ge(ml_p, N_ML - 1 + m)
                    else:
                        pe.wait_ge(sm_masked, m - 1)
                    nc.tensor.matmul(ps[:, 2 + m % 2, :(j + 1) * P], sm_qk[grp][b:b + DK, h // 2, j * P:(j + 1) * P],
                                     sm_qk[grp][b:b + DK, 2 + h // 2, :(j + 1) * P], start=True,
                                     stop=True).then_inc(sc_done, 1)

                def sm_turn(m):
                    j = m // HEADS % NT
                    pe.wait_ge(exp_done, m + 1)
                    if m < 2:
                        pe.wait_ge(decay_done, N_ML)
                    else:
                        pe.wait_ge(pt_out, m - 1)
                    for i in range(j + 1):
                        ins = nc.tensor.transpose(ps[:, 4 + m % 2, i * P:(i + 1) * P],
                                                  sbuf_p[:, m % 2, i * P:(i + 1) * P], ident[:])
                    ins.then_inc(pt_done, 1)

                def sm_values(m):
                    k, h = divmod(m, HEADS)
                    grp, j = divmod(k, NT)
                    pe.wait_ge(pt_out, m + 1)
                    if h == 0:
                        pe.wait_ge(tile_out, tiles_before(8 if grp == 0 else 11) + j + 1)
                        if k < 2:
                            pe.wait_ge(ml_fin, N_ML // 2 - 1 + k)
                        else:
                            pe.wait_ge(sm_fin, k - 1)
                    for i in range(j + 1):
                        ins = nc.tensor.matmul(ps[:, 6 + k % 2, h * DK:(h + 1) * DK],
                                               sbuf_pt[:, m % 2, i * P:(i + 1) * P],
                                               sm_v[:, i, HEADS * grp + h, :], start=(i == 0), stop=(i == j))
                    ins.then_inc(pv_done, 1)

                def head_step(n):
                    if n < N_ML:
                        if n % HEADS == 0:
                            ml_spread(n // HEADS)
                        ml_scores(n)
                    elif n < N_TASKS:
                        sm_scores(n - N_ML)
                    if N_ML < n <= N_TASKS:
                        sm_turn(n - 1 - N_ML)
                    if 2 <= n < N_ML + 2:
                        ml_values(n - 2)
                    elif n >= N_ML + 2:
                        sm_values(n - 2 - N_ML)

                pe.wait_ge(nlo_done, 8)
                for j in range(IDX_FROM):
                    for part in range(PARTS):
                        unit_part(j, part)
                    if j == 0:
                        pe.wait_ge(params_loaded, 64)
                        nc.tensor.transpose(ps[:, 4, 0:16], conv_rows[:], ident[0:16, 0:16]).then_inc(conv_t, 1)
                    if j == 3:
                        pe.wait_ge(gate_step, 7)
                        pe.wait_ge(iw_scaled, 1)
                        pe.wait_ge(conv_w_ready, 1)
                        for t in range(NT):
                            ins = nc.tensor.transpose(ps[:, 4, t * 68:(t + 1) * 68],
                                                      rows_t[0:68, t * P:(t + 1) * P], ident[0:68, 0:68])
                        ins.then_inc(rows_turned, 1)
                for j in range(IDX_FROM, N_PROJ):
                    for part in range(PARTS):
                        unit_part(j, part)
                        if j < HEAD_FROM:
                            index_scores((j - IDX_FROM) * PARTS + part)
                        else:
                            head_step((j - HEAD_FROM) * PARTS + part)

                def mix_turn(n):
                    c, i = divmod(n, NT)
                    for q in range(4):
                        k = 4 * c + q
                        ins = nc.tensor.transpose(ps[:, n, q * P:(q + 1) * P], Y[:, i, k * P:(k + 1) * P], ident[:])
                    ins.then_inc(nt_done, 1)

                head_step(N_TASKS)
                pe.wait_ge(tile_out, tiles_before(N_PROJ))
                pe.wait_ge(sm_masked, N_SM)
                for i in range(NT):
                    pe.wait_ge(ml_out, NT + i + 1)
                    mix_turn(i)
                    if i == 0:
                        head_step(N_TASKS + 1)
                for i in range(NT):
                    if i == 0:
                        pe.wait_ge(pt_out, N_SM)
                    pe.wait_ge(sm_fin, NT + i + (2 if i == 2 else 1))
                    mix_turn(NT + i)
                for j in range(N_PROJ, N_PRE):
                    pe.wait_ge(lo_ready, j + 1)
                    hi, lo = slot(w_hi, j, "out"), slot(w_lo, j, "out")
                    for t in range(NT):
                        if j == N_PROJ:
                            pe.wait_ge(nlo_done, 8 + 2 * (t + 1))
                        s = slice(t * P, (t + 1) * P)
                        for c in range(2):
                            for k in range(2):
                                kk = 2 * (j - N_PROJ) + k
                                cs = slice(c * 512, (c + 1) * 512)
                                ins = passes(ps[:, 2 * t + c, :], (hT_hi[:, kk, s], hT_lo[:, kk, s]),
                                             (hi[:, k, cs], lo[:, k, cs]), kk == 0, kk == KD - 1)
                        ins.then_inc(mm_done, 1)
                for i in range(NT):
                    pe.wait_ge(xn_done, NT + i + 1)
                    turn(2, i)
                pe.wait_ge(nlo_done, 24)

                with pe.Fori(0, GROUPS) as g:
                    for jj in range(GU):
                        pe.wait_ge(lo_ready, g * GU + (N_PRE + jj + 1))
                        if jj < 4:
                            hi, lo = slot(w_hi, jj, "in"), slot(w_lo, jj, "in")
                            for t in range(2):
                                m = 2 * jj + t
                                pe.wait_ge(y_out, g * 8 + m + 1)
                                s = slice(t * P, (t + 1) * P)
                                for k in range(KD):
                                    ins = passes(ps[:, m, :], (hi[:, k, s], lo[:, k, s]),
                                                 (hT_hi[:, k, :], hT_lo[:, k, :]), k == 0, k == KD - 1)
                                ins.then_inc(mm_done, 1)
                        else:
                            c, kh = (jj - 4) // 2, jj % 2
                            hi, lo = slot(w_hi, jj, "t"), slot(w_lo, jj, "t")
                            if jj < 6:
                                pe.wait_ge(hid_ready, g * HID + (4 * kh + 4 + 2))
                            for t in range(NT):
                                s = slice(t * P, (t + 1) * P)
                                for k in range(4):
                                    kk = 4 * kh + k
                                    ins = passes(ps[:, 4 * c + t, :], (hid_hi[:, kk, s], hid_lo[:, kk, s]),
                                                 (hi[:, k, :], lo[:, k, :]), kk == 0, kk == HID - 1)
                                ins.then_inc(mm_done, 1)
                pe.wait_ge(mm_done, EV_MLP + GROUPS * GROUP_EVENTS)
                pe.sem_inc(layer_end, 1)


def unit_end(g, jj):
    if jj >= 0:
        return mlp_event(g, jj, 1 if jj < 4 else 3)
    return g * GROUP_EVENTS + (EV_MLP + 4 * (jj + 1))


_INS = ["x", "norm_mix_pre", "w_in", "ml_conv", "ml_i_bias", "ml_f_bias", "ml_head_norm", "w_out",
        "norm_mix_post", "norm_mlp_pre", "w_ff1", "w_ff2", "norm_mlp_post"]


def kernel(**inputs):
    import numpy as np
    import concourse.bacc as bacc
    from concourse.bass_utils import run_bass_kernel_spmd

    nc = bacc.Bacc("TRN2", target_bir_lowering=False, num_devices=1)
    arrays, args = {}, []
    for name in _INS:
        a = np.ascontiguousarray(inputs[name])
        arrays[f"in_{name}"] = a
        args.append(nc.dram_tensor(f"in_{name}", a.shape, mybir.dt.from_np(a.dtype), kind="ExternalInput").ap())
    shape = (1, SEQ, D)
    args.append(nc.dram_tensor("out_x", shape, F32, kind="ExternalOutput").ap())
    trunk(nc, *args)
    r = run_bass_kernel_spmd(nc, [arrays], core_ids=[0])
    return r.results[0]["out_x"]
```

```python
from contextlib import ExitStack

import concourse.bass as bass
from concourse import mybir

F32 = mybir.dt.float32
F32R = mybir.dt.float32r
ALU = mybir.AluOpType
ACT = mybir.ActivationFunctionType
AX = mybir.AxisListType

P = 128
DEPTH, SEQ, D = 2, 512, 1024
NT = SEQ // P
KD = D // P
HEADS, DK, ML_DV = 4, 64, 128
TOPK = min(256, SEQ // 4)
D_FF = 4 * D
EPS = 1e-6
W_QK, W_V, W_SM = HEADS * DK, HEADS * ML_DV, HEADS * DK
(C_MLQ, C_MLK, C_MLV, C_MLO, C_I, C_F, C_MBQ, C_MBK, C_MBV, C_DSQ, C_DSK, C_DSV, C_IXQ, C_IXK, C_IXW) = (
    0, 256, 512, 1024, 1536, 1540, 1544, 1800, 2056, 2312, 2568, 2824, 3080, 3336, 3400)

UNIT = 2048
UNITS = [("t", C_MLV), ("t", C_MLV + 256), ("small", None), ("f", C_IXQ), ("f", C_MLK), ("f", C_MLQ),
         ("f", C_MBQ), ("f", C_MBK), ("t", C_MBV), ("f", C_DSQ), ("f", C_DSK), ("t", C_DSV),
         ("t", C_MLO), ("t", C_MLO + 256)]
N_PROJ = len(UNITS)
N_OUT = 4
N_PRE = N_PROJ + N_OUT
GROUPS = 4
HID = D_FF // GROUPS // P
GU = 8

PARTS = 6
IDX_FROM = 4
HEAD_FROM = 6
CONV_CHUNK = (2, 3, 0, 1)
CONV_AT = [(4, 5), (5, 1), (5, 3), (6, 0)]
SILU_AT = [(5, 0), (5, 2), (5, 4), (6, 0)]
WARM = 56
N_IDX = (NT - 1) * HEADS
N_ML = NT * HEADS
N_SM = 2 * NT * HEADS
N_TASKS = N_ML + N_SM
assert (HEAD_FROM - IDX_FROM) * PARTS == N_IDX and (N_PROJ - HEAD_FROM) * PARTS == N_TASKS

MASKED = -1e30
ABSENT, TAKEN = -2e38, -3e38
SCORE_AT = {1: 0, 2: 256, 3: 640}

NORMS = ([(0, i) for i in range(NT)],
         [(1, 0), (1, 1), (2, 0), (2, 1), (1, 2), (1, 3), (2, 2), (2, 3)] + [(3, i) for i in range(NT)])
NORM_PART = {k: part for part in (0, 1) for k in NORMS[part]}
NORM_AT = {k: n + 1 for part in (0, 1) for n, k in enumerate(NORMS[part])}


def tiles_of(j):
    return {"t": 4, "f": 2, "small": 1}[UNITS[j][0]] if j < N_PROJ else 4


def tiles_before(j):
    return sum(tiles_of(i) for i in range(j))


PROJ_TILES = tiles_before(N_PROJ)


def tiles_in_part(j, part):
    n = tiles_of(j)
    return range(part * n // PARTS, (part + 1) * n // PARTS)


N_LATE = N_OUT + GROUPS * GU
GROUP_EVENTS = 4 * 2 + 4 * 4
EV_MLP = N_OUT * NT
LATE_EVENTS = EV_MLP + GROUPS * GROUP_EVENTS


def mlp_event(g, jj, t):
    before = 2 * jj if jj < 4 else 8 + 4 * (jj - 4)
    return g * GROUP_EVENTS + (EV_MLP + before + t + 1)


def unit_end(g, jj):
    if jj >= 0:
        return mlp_event(g, jj, 1 if jj < 4 else 3)
    return g * GROUP_EVENTS + (EV_MLP + 4 * (jj + 1))


def dmas_of(j):
    return 4 if UNITS[j][0] == "small" else 1


def raw_landed(j):
    if j >= N_PROJ:
        return 16 * ((j - N_PROJ) // 2 + 1)
    return 16 * sum(dmas_of(i) for i in range(j % 2, j + 1, 2))


OUT_ORDER = [(0, 0), (1, 0), (0, 1), (1, 1), (0, 2), (0, 3), (1, 2), (1, 3),
             (2, 0), (2, 1), (3, 0), (3, 1), (2, 2), (2, 3), (3, 2), (3, 3)]


def out_event(j, t):
    return OUT_ORDER.index((j, t)) + 1


def out_unit_end(j):
    return max(out_event(j, t) for t in range(NT))


RAW_OUT = 16 * N_OUT // 2


def trunk(nc, x, norm_mix_pre, w_in, ml_conv, ml_i_bias, ml_f_bias, ml_head_norm, w_out,
          norm_mix_post, norm_mlp_pre, w_ff1, w_ff2, norm_mlp_post, out):
    ctx = ExitStack()
    with ctx:
        def sb(name, shape, dt=F32, on=ctx):
            return on.enter_context(nc.sbuf_tensor(name, shape, dt))

        X = sb("X", [P, NT, D])
        Y = sb("Y", [P, NT, D])
        gain_pre = sb("gain_pre", [P, D])
        gain_post = sb("gain_post", [P, D])
        head_gain = sb("head_gain", [P, W_V])
        raw = sb("raw", [P, 2, UNIT])
        w_hi = sb("w_hi", [P, 2, UNIT], F32R)
        w_lo = sb("w_lo", [P, 2, UNIT], F32R)
        hT_hi = sb("hT_hi", [P, KD, SEQ], F32R)
        hT_lo = sb("hT_lo", [P, KD, SEQ], F32R)
        sbuf_s = sb("scores", [P, 2, SEQ])
        sbuf_p = sb("probs", [P, 2, SEQ])
        sbuf_pt = sb("probs_t", [P, 2, SEQ])
        sq = sb("squares", [P, 2 * ML_DV])
        with ExitStack() as shared:
            hid_hi = sb("hid_hi", [P, HID, SEQ], F32R, shared)
            hid_lo = sb("hid_lo", [P, HID, SEQ], F32R, shared)
            hid_r = sb("hid_r", [P, 2, SEQ], on=shared)
            hid_h = sb("hid_h", [P, 2, SEQ], on=shared)
        ml_qk = sb("ml_qk", [P, 4, SEQ])
        sm_qk = [sb("mb_qk", [P, 4, SEQ]), sb("ds_qk", [P, 4, SEQ])]
        ix_q = sb("ix_q", [P, 2, SEQ])
        ix_k = sb("ix_k", [P, SEQ])
        ml_gate = sb("ml_gate", [P, NT, W_V])
        sb("pad_m", [P, (2 * HID + 4) * SEQ - 15 * SEQ - NT * W_V])
        rows_t = sb("rows_t", [P, SEQ])
        ml_v = sb("ml_v", [P, NT, HEADS, ML_DV + 1])
        sm_v = sb("sm_v", [P, NT, 2 * HEADS, DK])
        score = sb("score", [P, 1152])
        causal = sb("causal", [P, SEQ])
        ones = sb("ones", [HEADS, SEQ])
        ident = sb("ident", [P, P])
        pick = sb("pick", [HEADS, HEADS, P])
        half = sb("half", [P, HEADS])
        conv_rows = sb("conv_rows", [16, P])
        conv_w = sb("conv_w", [P, 16])
        gate_bias = sb("gate_bias", [P, 1])
        a_col = sb("a_col", [P, NT, HEADS])
        expm = sb("expm", [P, NT, HEADS])
        iw_col = sb("iw_col", [P, NT, HEADS])
        ms = sb("ms", [P, 16])
        ms_eps = sb("ms_eps", [P, 16])
        rstd = sb("rstd", [P, 16])
        hms = sb("hms", [P, NT, HEADS])
        hms_eps = sb("hms_eps", [P, NT, HEADS])
        hrstd = sb("hrstd", [P, NT, HEADS])
        den = sb("den", [P, NT, HEADS])
        rden = sb("rden", [P, NT, HEADS])
        top8 = sb("top8", [P, 8])
        nmin = sb("nmin", [P, 2])
        sums = sb("sums", [P, 2, HEADS])
        rsum = sb("rsum", [P, 2, HEADS])
        sq_sink = sb("sq_sink", [P, D], mybir.dt.bfloat16)
        rows = sbuf_pt[:, 0, :]
        relu_s = sbuf_p
        gained = [hid_r[:].rearrange("p a b -> p (a b)"), hid_h[:].rearrange("p a b -> p (a b)")]
        conv_in = Y[:, 0, :].rearrange("p (b t) -> p b t", b=2)
        conv_acc = Y[:, 1, :].rearrange("p (b t) -> p b t", b=2)
        g_f, g_n = Y[0:HEADS, 2, 0:SEQ], Y[0:HEADS, 2, SEQ:2 * SEQ]
        g_B, g_M = Y[0:HEADS, 3, 0:SEQ], Y[0:HEADS, 3, SEQ:2 * SEQ]

        ps = ctx.enter_context(nc.psum_tensor("ps", [P, 8, 512], F32))

        early, late, standing = [], [], []

        def sem(name, of):
            h = ctx.enter_context(nc.semaphore(name))
            of.append(h.num)
            return h

        x_loaded = [sem(f"x{i}_loaded", standing) for i in range(NT)]
        stored = sem("stored", standing)
        table_loaded = sem("table_loaded", standing)
        const_step = sem("const_step", standing)
        part_go = [sem("early_go", standing), sem("late_go", standing)]
        part_begun = sem("part_begun", standing)

        names = """part_over raw0_loaded raw1_loaded gain_pre_loaded hi_ready lo_ready mm_done ms_done eps_done
            rstd_done xn_done nt_done nhi_done nlo_done""".split()
        E = {n: sem(n + "_early", early) for n in names}
        (params_loaded, conv_t, conv_w_ready, tile_out, conv_step, silu_done, gate_step, softplus_done, iw_copied,
         rows_turned, cols_done, idx_done, idx_relu, idx_acc, score_ready, tk, spread_done, st_done, decay_done,
         decay_cut, ml_p, ml_pv, ml_step, ml_fin, hms_done, hms_eps_done, hrstd_done, ml_gained, gate_done,
         ml_out, sc_done, sm_masked, exp_done, pt_done, pt_out, pv_done, rsum_done, sm_fin) = (
            sem(n, early) for n in """params_loaded conv_t conv_w_ready tile_out conv_step silu_done gate_step
            softplus_done iw_copied rows_turned cols_done idx_done idx_relu idx_acc score_ready topk_step spread_done
            st_done decay_done decay_cut ml_p ml_pv ml_step ml_fin hms_done hms_eps_done hrstd_done ml_gained
            gate_done ml_out sc_done sm_masked exp_done pt_done pt_out pv_done rsum_done sm_fin""".split())
        L = {n: sem(n + "_late", late) for n in names}
        gain_post_loaded, applied_t, applied, hid_relu, hid_sq, hid_hi_done, hid_ready, y_zero, y_out = (
            sem(n, late) for n in """gain_post_loaded applied_t applied hid_relu hid_sq hid_hi_done hid_ready
            y_zero y_out""".split())
        assert late == list(range(late[0], late[-1] + 1)) and early == list(range(early[0], early[-1] + 1))
        part_over, gain_pre_loaded, hi_ready, lo_ready, mm_done, ms_done, eps_done, rstd_done, xn_done, nt_done, (
            nhi_done), nlo_done = ([E[n], L[n]] for n in names if not n.startswith("raw"))
        raw_loaded = [[E["raw0_loaded"], E["raw1_loaded"]], [L["raw0_loaded"], L["raw1_loaded"]]]

        SLOTW = {"in": (8, 256), "t": (4, 512), "out": (2, 1024)}

        def slot(t, j, form):
            k, n = SLOTW[form]
            return t[:, j % 2, :].rearrange("p (k n) -> p k n", k=k)

        def mask_of(grp, j):
            n = (j + 1) * P
            if grp == 0 or j == 0:
                return causal[:, SEQ - n:SEQ]
            return score[:, SCORE_AT[j]:SCORE_AT[j] + n]

        def begin(eng, part, l):
            eng.wait_ge(part_go[part], l + 1)
            eng.sem_inc(part_begun, 1)
            eng.wait_ge(part_go[part], 1)

        block = ctx.enter_context(nc.Block())

        @block.sync
        def _(sp):
            sp.dma_start(X[:, 0], x[0, 0:P]).then_inc(x_loaded[0], 16)

            with sp.Fori(0, DEPTH) as l:
                begin(sp, 0, l)

                def load(dst, src, s):
                    sp.dma_start(dst, src).then_inc(s, 16)

                def load_unit(j):
                    s = raw_loaded[j >= N_PROJ][j % 2]
                    if j < 2:
                        sp.wait_ge(lo_ready[1], N_LATE - 1 + j)
                    elif j < N_PROJ + 2:
                        sp.wait_ge(lo_ready[0], j - 1)
                    else:
                        sp.wait_ge(lo_ready[1], j - 1 - N_PROJ)
                    if j >= N_PROJ:
                        r = (j - N_PROJ) * 2 * P
                        load(slot(raw, j, "out"), w_out[l, r:r + 2 * P, :].rearrange("(k p) n -> p k n", p=P), s)
                        return
                    w = w_in[l].rearrange("(k p) n -> p k n", p=P)
                    u = UNITS[j]
                    if u[0] != "small":
                        load(slot(raw, j, "in"), w[:, :, u[1]:u[1] + 256], s)
                    else:
                        d = slot(raw, j, "in")
                        for at, c, n in ((0, C_IXK, DK), (DK, C_I, HEADS), (DK + HEADS, C_IXW, HEADS),
                                         (DK + 32, C_F, HEADS)):
                            load(d[:, :, at:at + n], w[:, :, c:c + n], s)

                sp.wait_ge(xn_done[1], NT)
                load(gain_pre[:], norm_mix_pre[l][None, :].to_broadcast([P, D]), gain_pre_loaded[0])
                load_unit(0)
                sp.wait_ge(x_loaded[2], 16)
                load_unit(1)
                load(conv_rows[:], ml_conv[l].rearrange("k (c p) -> (k c) p", p=P), params_loaded)
                load(gate_bias[0:HEADS, :], ml_i_bias[l][:, None], params_loaded)
                load(gate_bias[32:32 + HEADS, :], ml_f_bias[l][:, None], params_loaded)
                load(head_gain[:], ml_head_norm[l][None, :].to_broadcast([P, W_V]), params_loaded)
                for j in range(2, N_PRE):
                    if j == 4:
                        sp.wait_ge(applied, 2 * NT)
                        sp.sem_inc(part_over[1], 1)
                        begin(sp, 1, l)
                        load(gain_post[:], norm_mix_post[l][None, :].to_broadcast([P, D]), gain_post_loaded)
                        sp.wait_ge(xn_done[0], NT)
                        load(gain_pre[:], norm_mlp_pre[l][None, :].to_broadcast([P, D]), gain_pre_loaded[1])
                    load_unit(j)
                    if j == N_PROJ + 1:
                        sp.sem_inc(part_over[0], 1)
                with sp.Fori(0, GROUPS) as g:
                    for jj in range(GU):
                        sp.wait_ge(lo_ready[1], g * GU + (N_OUT + jj - 1))
                        sp.wait_ge(x_loaded[0], 16)
                        if jj < 4:
                            src = w_ff1[l].rearrange("(k p) n -> p k n", p=P)[
                                :, :, bass.ds(g * (HID * P) + jj * 256, 256)]
                            load(slot(raw, jj, "in"), src, raw_loaded[1][jj % 2])
                        else:
                            c, half_k = (jj - 4) // 2, jj % 2
                            src = w_ff2[l, bass.ds(g * (HID * P) + half_k * 4 * P, 4 * P), c * 512:(c + 1) * 512]
                            load(slot(raw, jj, "t"), src.rearrange("(k p) n -> p k n", p=P), raw_loaded[1][jj % 2])
                sp.wait_ge(applied, NT)
                load(gain_post[:], norm_mlp_post[l][None, :].to_broadcast([P, D]), gain_post_loaded)
                sp.wait_ge(gain_post_loaded, 32)
            for i in range(NT):
                sp.wait_ge(applied, NT + i + 1)
                sp.dma_start(out[0, i * P:(i + 1) * P], X[:, i]).then_inc(stored, 16)
            sp.wait_ge(stored, 16 * NT)

        def head_pair(pool, p):
            j, a = p // 2, 2 * (p % 2)
            y = Y[:, j, a * ML_DV:(a + 2) * ML_DV]
            pool.wait_ge(hms_done, p + 1)
            nc.gpsimd.tensor_scalar(hms_eps[:, j, a:a + 2], hms[:, j, a:a + 2], 1.0 / ML_DV, EPS, ALU.mult,
                                    ALU.add).then_inc(hms_eps_done, 1)
            nc.gpsimd.tensor_tensor(y, y, head_gain[:, a * ML_DV:(a + 2) * ML_DV], ALU.mult).then_inc(ml_gained, 1)
            pool.wait_ge(hms_eps_done, p + 1)
            nc.gpsimd.tensor_tensor(hrstd[:, j, a:a + 2], hms_eps[:, j, a:a + 2], half[:, 0:2],
                                    ALU.pow).then_inc(hrstd_done, 1)

        @block.gpsimd
        def _(pool):
            steps = [0]

            def step(ins):
                steps[0] += 1
                ins.then_inc(const_step, 1)
                pool.wait_ge(const_step, steps[0])

            step(pool.memset(half[:], -0.5))
            for s, n in ((lo_ready[1], N_LATE), (xn_done[1], NT), (applied, 2 * NT), (mm_done[1], LATE_EVENTS),
                         (y_out, 8 * GROUPS + 8)):
                pool.sem_inc(s, n)
            pool.sem_inc(part_go[0], 1)
            step(pool.memset(ident[:], 0.0))
            step(pool.affine_select(out=ident[:], in_=ident[:], compare_op=ALU.not_equal, fill=1.0, base=0,
                                    pattern=[[-1, P]], channel_multiplier=1))
            step(pool.memset(pick[:], 1.0))
            step(pool.affine_select(out=pick[:], in_=pick[:], compare_op=ALU.is_equal, fill=0.0, base=0,
                                    pattern=[[-1, HEADS], [0, P]], channel_multiplier=1))
            step(pool.memset(causal[:], 0.0))
            step(pool.affine_select(out=causal[:, SEQ - P:SEQ], in_=causal[:, SEQ - P:SEQ], compare_op=ALU.is_ge,
                                    fill=MASKED, base=0, pattern=[[-1, P]], channel_multiplier=1))
            step(pool.memset(ones[:], 1.0))
            step(pool.memset(rows_t[:], 0.0))
            step(pool.memset(ml_v[:], 1.0))

            with pool.Fori(0, DEPTH) as l:
                def make_rstd(norm, i):
                    n, part = NORM_AT[norm, i], NORM_PART[norm, i]
                    c = slice(NT * norm + i, NT * norm + i + 1)
                    pool.wait_ge(ms_done[part], n)
                    nc.gpsimd.tensor_scalar(ms_eps[:, c], ms[:, c], EPS, None, ALU.add).then_inc(eps_done[part], 1)
                    pool.wait_ge(eps_done[part], n)
                    nc.gpsimd.tensor_tensor(rstd[:, c], ms_eps[:, c], half[:, 0:1],
                                            ALU.pow).then_inc(rstd_done[part], 1)

                for norm, i in NORMS[0]:
                    make_rstd(norm, i)
                pool.wait_ge(part_over[1], 4)
                pool.sem_clear(range(late[0], late[-1] + 1))
                pool.sem_inc(part_go[1], 1)
                for j in range(1, NT):
                    pool.wait_ge(idx_acc, HEADS * j)
                    d = score[:, SCORE_AT[j] + j * P:SCORE_AT[j] + (j + 1) * P]
                    nc.gpsimd.affine_select(out=d, in_=d, compare_op=ALU.is_ge, fill=ABSENT, base=0,
                                            pattern=[[-1, P]], channel_multiplier=1).then_inc(score_ready, 1)
                pool.wait_ge(params_loaded, 64)
                for n in range(N_ML):
                    j = n // HEADS
                    pool.wait_ge(decay_done, n + 1)
                    d = sbuf_s[:, n % 2, j * P:(j + 1) * P]
                    nc.gpsimd.affine_select(out=d, in_=d, compare_op=ALU.is_ge, fill=0.0, base=0,
                                            pattern=[[1, P]], channel_multiplier=-1).then_inc(decay_cut, 1)
                    if n >= 5 and n % 2:
                        head_pair(pool, (n - 5) // 2)
                for p in range(N_ML // 2 - 2, N_ML // 2):
                    head_pair(pool, p)
                pool.wait_ge(part_over[0], 4)
                pool.sem_clear(range(early[0], early[-1] + 1))
                pool.sem_inc(part_go[0], 1)
                for norm, i in NORMS[1]:
                    if (norm, i) == (3, 0):
                        pool.wait_ge(nt_done[1], 8)
                        for t in range(NT):
                            nc.gpsimd.memset(Y[:, t], 0.0).then_inc(y_zero, 1)
                    make_rstd(norm, i)
                pool.wait_ge(rstd_done[1], len(NORMS[1]))

        @block.scalar
        def _(act):
            act.wait_ge(const_step, 1)
            nc.scalar.activation(sq_sink[:, 0:1], half[:, 0:1], ACT.Square).then_inc(table_loaded, 1)
            act.wait_ge(table_loaded, 1)
            act.wait_ge(x_loaded[0], 16)
            for i in range(1, NT):
                act.dma_start(X[:, i], x[0, i * P:(i + 1) * P]).then_inc(x_loaded[i], 16)
            with act.Fori(0, DEPTH) as l:
                begin(act, 0, l)

                def mean_square(norm, i, src):
                    n, part = NORM_AT[norm, i], NORM_PART[norm, i]
                    if n >= 2:
                        act.wait_ge(ms_done[part], n - 1)
                    c = NT * norm + i
                    nc.scalar.activation(sq_sink[:], src, ACT.Square, scale=D ** -0.5,
                                         accum_out=ms[:, c:c + 1]).then_inc(ms_done[part], 1)

                def split_hi(j):
                    part = j >= N_PROJ
                    act.wait_ge(raw_loaded[part][j % 2], raw_landed(j))
                    if j < 2:
                        act.wait_ge(mm_done[1], LATE_EVENTS - 4 * (1 - j))
                    elif j < N_PROJ + 2:
                        act.wait_ge(mm_done[0], tiles_before(j - 1))
                    else:
                        act.wait_ge(mm_done[1], out_unit_end(j - 2 - N_PROJ))
                    nc.scalar.copy(w_hi[:, j % 2], raw[:, j % 2]).then_inc(hi_ready[part], 1)

                def split_hi_mlp(g, jj):
                    act.wait_ge(raw_loaded[1][jj % 2], g * 64 + (RAW_OUT + 16 * (jj // 2 + 1)))
                    act.wait_ge(mm_done[1], unit_end(g, jj - 2))
                    nc.scalar.copy(w_hi[:, jj % 2], raw[:, jj % 2]).then_inc(hi_ready[1], 1)

                def norm_hi(stage, i):
                    for c in range(2):
                        act.wait_ge(nt_done[stage], 2 * i + c + 1)
                        nc.scalar.copy(hT_hi[:, 4 * c:4 * c + 4, i * P:(i + 1) * P],
                                       ps[:, 2 * i + c, :].rearrange("p (k t) -> p k t", k=4)).then_inc(nhi_done[stage], 1)

                for i in range(NT):
                    act.wait_ge(x_loaded[i], 16)
                    act.wait_ge(applied, NT + i + 1)
                    mean_square(0, i, X[:, i])
                    if i == 0:
                        split_hi(0)
                    elif i < NT - 1:
                        norm_hi(0, i - 1)
                split_hi(1)
                norm_hi(0, NT - 2)
                def tile_copy(j, t):
                    kind, col = UNITS[j]
                    x = tiles_before(j) + t
                    act.wait_ge(mm_done[0], x + 1)
                    if kind == "t":
                        src = ps[:, x % 2, 0:256]
                        if col in (C_MLV, C_MLV + 256):
                            h = (col - C_MLV) // ML_DV
                            ins = nc.scalar.copy(ml_v[:, t, h:h + 2, 0:ML_DV], src.rearrange("p (h e) -> p h e", h=2))
                        elif col in (C_MLO, C_MLO + 256):
                            ins = nc.scalar.copy(ml_gate[:, t, col - C_MLO:col - C_MLO + 256], src)
                        else:
                            h = HEADS * (col == C_DSV)
                            ins = nc.scalar.copy(sm_v[:, t, h:h + HEADS], src.rearrange("p (h e) -> p h e", h=HEADS))
                    else:
                        src = ps[:, x % 2, :]
                        if kind == "small":
                            nc.scalar.copy(rows[0:36, :], src[DK:DK + 36, :])
                            nc.scalar.copy(ix_k[0:DK, :], src[0:DK, :])
                            ins = nc.scalar.copy(ix_k[DK:2 * DK, :], src[0:DK, :])
                        elif col in (C_MLQ, C_MLK):
                            if col == C_MLQ:
                                act.wait_ge(conv_step, 4 * (t + 1))
                            ins = nc.scalar.copy(conv_in[:, t], src)
                        else:
                            dst, at = {C_IXQ: (ix_q, 0), C_MBQ: (sm_qk[0], 0), C_MBK: (sm_qk[0], 2),
                                       C_DSQ: (sm_qk[1], 0), C_DSK: (sm_qk[1], 2)}[col]
                            ins = nc.scalar.copy(dst[:, at + t], src)
                    ins.then_inc(tile_out, 1)

                tile_copy(0, 0)
                norm_hi(0, NT - 1)
                act.sem_inc(part_over[1], 1)

                def index_relu(n):
                    j, h = n // HEADS + 1, n % HEADS
                    act.wait_ge(idx_done, n + 1)
                    if n >= 2:
                        act.wait_ge(idx_acc, n - 1)
                    nc.scalar.activation(relu_s[:, n % 2, :(j + 1) * P], ps[:, 2 + n % 2, :(j + 1) * P],
                                         ACT.Relu).then_inc(idx_relu, 1)

                def decay(n):
                    j, h = divmod(n, HEADS)
                    if h == 0:
                        act.wait_ge(spread_done, j + 1)
                        act.wait_ge(cols_done, 3)
                    if n >= 2:
                        act.wait_ge(ml_p, n - 1)
                    for i in range(j + 1):
                        ins = nc.scalar.activation(sbuf_s[:, n % 2, i * P:(i + 1) * P],
                                                   ps[:, 4 + j % 2, h * P:(h + 1) * P], ACT.Exp,
                                                   bias=a_col[:, i, h:h + 1], scale=-1.0)
                    ins.then_inc(decay_done, 1)

                def sm_exp(m):
                    k, h = divmod(m, HEADS)
                    w = (k % NT + 1) * P
                    act.wait_ge(sm_masked, m + 1)
                    if m >= 2:
                        act.wait_ge(pt_done, m - 1)
                    if h == 0 and k >= 2:
                        act.wait_ge(rsum_done, k - 1)
                    nc.scalar.activation(sbuf_p[:, m % 2, :w], sbuf_s[:, m % 2, :w], ACT.Exp,
                                         bias=nmin[:, m % 2:m % 2 + 1], scale=-1.0,
                                         accum_out=sums[:, k % 2, h:h + 1]).then_inc(exp_done, 1)

                def pt_copy(m):
                    w = (m // HEADS % NT + 1) * P
                    act.wait_ge(pt_done, m + 1)
                    if m >= 2:
                        act.wait_ge(pv_done, m - 1)
                    nc.scalar.copy(sbuf_pt[:, m % 2, :w], ps[:, 4 + m % 2, :w]).then_inc(pt_out, 1)

                def head_step(n):
                    if n < N_ML:
                        decay(n)
                    elif n < N_TASKS:
                        sm_exp(n - N_ML)
                    if n > N_ML:
                        pt_copy(n - 1 - N_ML)

                for j in range(IDX_FROM):
                    for t in range(j == 0, tiles_of(j)):
                        tile_copy(j, t)
                    split_hi(j + 2)
                    if j == 2:
                        act.wait_ge(tile_out, tiles_before(3))
                        nc.scalar.copy(rows_t[0:2 * HEADS, :], rows[0:2 * HEADS, :]).then_inc(iw_copied, 1)
                        act.wait_ge(gate_step, 2)
                        nc.scalar.activation(g_n, g_n, ACT.Exp).then_inc(softplus_done, 1)
                        act.wait_ge(softplus_done, 1)
                        nc.scalar.activation(g_n, g_n, ACT.Ln, bias=1.0).then_inc(softplus_done, 1)
                for j in range(IDX_FROM, N_PROJ):
                    for part in range(PARTS):
                        for t in tiles_in_part(j, part):
                            tile_copy(j, t)
                        if part == PARTS - 1:
                            if j == N_PROJ - 2:
                                begin(act, 1, l)
                            split_hi(j + 2)
                        for o, at in enumerate(SILU_AT):
                            if at == (j, part):
                                act.wait_ge(conv_step, 4 * (o + 1))
                                nc.scalar.activation(ml_qk[:, CONV_CHUNK[o]], conv_acc[:, o % 2],
                                                     ACT.Silu).then_inc(silu_done, 1)
                        if j < HEAD_FROM:
                            index_relu((j - IDX_FROM) * PARTS + part)
                            if (j, part) == (IDX_FROM, 1):
                                act.wait_ge(rows_turned, 1)
                                r = ps[:, 4, 0:NT * 36].rearrange("p (t c) -> p t c", t=NT)
                                nc.scalar.copy(a_col[:], r[:, :, 0:HEADS]).then_inc(cols_done, 1)
                                nc.scalar.mul(iw_col[:], r[:, :, HEADS:2 * HEADS], (HEADS * DK) ** -0.5).then_inc(cols_done, 1)
                                nc.scalar.activation(expm[:], r[:, :, 32:32 + HEADS], ACT.Exp, scale=-1.0).then_inc(cols_done, 1)
                        else:
                            head_step((j - HEAD_FROM) * PARTS + part)
                for t in range(NT):
                    act.wait_ge(tile_out, tiles_before(N_PROJ - 1) + t + 1)
                    nc.scalar.activation(ml_gate[:, t], ml_gate[:, t], ACT.Sigmoid).then_inc(gate_done, 1)
                    if t == 0:
                        head_step(N_TASKS)

                for n in range(2 * NT):
                    c, i = divmod(n, NT)
                    act.wait_ge(nt_done[0], 8 + n + 1)
                    nc.scalar.copy(hT_hi[:, 4 * c:4 * c + 4, i * P:(i + 1) * P],
                                   ps[:, n, :].rearrange("p (k t) -> p k t", k=4)).then_inc(nhi_done[0], 1)
                act.sem_inc(part_over[0], 1)
                split_hi(N_PROJ + 2)
                split_hi(N_PROJ + 3)

                def mix_square(i):
                    act.wait_ge(mm_done[1], out_event(N_OUT - 1, i))
                    mean_square(1, i, ps[:, 2 * i:2 * i + 2, :].rearrange("p a b -> p (a b)"))

                def x_square(i):
                    act.wait_ge(applied, i + 1)
                    mean_square(2, i, X[:, i])

                mix_square(0)
                mix_square(1)
                x_square(0)
                x_square(1)
                act.wait_ge(raw_loaded[1][0], RAW_OUT + 16)
                act.wait_ge(mm_done[1], out_unit_end(2))
                nc.scalar.copy(w_hi[:, 0], raw[:, 0]).then_inc(hi_ready[1], 1)
                norm_hi(1, 0)
                mix_square(2)
                norm_hi(1, 1)
                mix_square(3)
                x_square(2)
                x_square(3)
                norm_hi(1, 2)
                norm_hi(1, 3)
                split_hi_mlp(0, 1)

                def hidden(g, m):
                    act.wait_ge(mm_done[1], mlp_event(g, m // 2, m % 2))
                    act.wait_ge(hid_ready, g * HID + m + 1)
                    nc.scalar.activation(hid_r[:, m % 2], ps[:, m, :], ACT.Relu).then_inc(hid_relu, 1)
                    act.wait_ge(hid_relu, g * HID + m + 1)
                    nc.scalar.activation(hid_hi[:, m], hid_r[:, m % 2], ACT.Square).then_inc(hid_hi_done, 1)

                def group(g, is_last):
                    for jj in range(GU):
                        if jj < 4:
                            hidden(g, 2 * jj)
                            hidden(g, 2 * jj + 1)
                        if jj + 2 < GU:
                            split_hi_mlp(g, jj + 2)
                        elif not is_last:
                            split_hi_mlp(g + 1, jj + 2 - GU)

                with act.Fori(0, GROUPS - 1) as g:
                    group(g, False)
                group(GROUPS - 1, True)
                for i in range(NT):
                    act.wait_ge(y_out, 8 * GROUPS + 8 + i - 3)
                    mean_square(3, i, Y[:, i])
                act.wait_ge(ms_done[1], len(NORMS[1]))

        @block.vector
        def _(dve):
            with dve.Fori(0, DEPTH) as l:
                begin(dve, 0, l)

                def split_lo_at(part, n, j):
                    dve.wait_ge(hi_ready[part], n + 1)
                    nc.vector.tensor_tensor(w_lo[:, j % 2], raw[:, j % 2], w_hi[:, j % 2].bitcast(F32),
                                            ALU.subtract).then_inc(lo_ready[part], 1)

                def split_lo(j):
                    split_lo_at(j >= N_PROJ, j - N_PROJ * (j >= N_PROJ), j)

                def normed(norm, i):
                    part = NORM_PART[norm, i]
                    dve.wait_ge(rstd_done[part], NORM_AT[norm, i])
                    dve.wait_ge(gain_pre_loaded[part], 16)
                    c = NT * norm + i
                    nc.vector.scalar_tensor_tensor(Y[:, i], X[:, i], rstd[:, c:c + 1], gain_pre[:], ALU.mult,
                                                   ALU.mult).then_inc(xn_done[part], 1)

                def norm_lo(stage, i):
                    for c in range(2):
                        dve.wait_ge(nhi_done[stage], 2 * i + c + 1)
                        nc.vector.tensor_tensor(
                            hT_lo[:, 4 * c:4 * c + 4, i * P:(i + 1) * P],
                            ps[:, 2 * i + c, :].rearrange("p (k t) -> p k t", k=4),
                            hT_hi[:, 4 * c:4 * c + 4, i * P:(i + 1) * P].bitcast(F32),
                            ALU.subtract).then_inc(nlo_done[stage], 1)

                def gain_on(norm, i, src, dst):
                    dve.wait_ge(gain_post_loaded, 16 if norm == 1 else 32)
                    nc.vector.tensor_tensor(dst, src, gain_post[:], ALU.mult).then_inc(applied_t, 1)

                def apply(norm, i, src):
                    n = i + 1 + (NT if norm == 3 else 0)
                    c = NT * norm + i
                    dve.wait_ge(rstd_done[1], NORM_AT[norm, i])
                    dve.wait_ge(applied_t, n)
                    nc.vector.scalar_tensor_tensor(X[:, i], src, rstd[:, c:c + 1], X[:, i], ALU.mult,
                                                   ALU.add).then_inc(applied, 1)

                dve.wait_ge(applied, 2 * NT)
                for i in range(NT):
                    normed(0, i)
                    if i == 0:
                        split_lo(0)
                    else:
                        norm_lo(0, i - 1)
                split_lo(1)
                norm_lo(0, NT - 1)
                dve.sem_inc(part_over[1], 1)

                def conv(o):
                    chunk = CONV_CHUNK[o]
                    acc, src = conv_acc[:, o % 2], conv_in[:, o % 2]
                    dve.wait_ge(tile_out, tiles_before(4) + o + 1)
                    dve.wait_ge(conv_w_ready, 1)
                    if o >= 2:
                        dve.wait_ge(silu_done, o - 1)
                    for n, k in enumerate((3, 2, 1, 0)):
                        w = conv_w[:, 4 * k + chunk:4 * k + chunk + 1]
                        d = 3 - k
                        if n == 0:
                            ins = nc.vector.tensor_scalar(acc, src, w, None, ALU.mult)
                        else:
                            dve.wait_ge(conv_step, 4 * o + n)
                            ins = nc.vector.scalar_tensor_tensor(acc[:, d:], src[:, :SEQ - d], w, acc[:, d:],
                                                                 ALU.mult, ALU.add)
                        ins.then_inc(conv_step, 1)

                def gates_f():
                    dve.wait_ge(params_loaded, 64)
                    dve.wait_ge(tile_out, tiles_before(3))
                    nc.vector.tensor_scalar(g_f, rows[32:32 + HEADS, :], gate_bias[32:32 + HEADS, :], None,
                                            ALU.add).then_inc(gate_step, 1)
                    dve.wait_ge(gate_step, 1)
                    nc.vector.scalar_tensor_tensor(g_n, g_f, -1.0, g_f, ALU.mult, ALU.min).then_inc(gate_step, 1)

                def gates_scan():
                    dve.wait_ge(softplus_done, 2)
                    nc.vector.scalar_tensor_tensor(g_f, g_f, 0.0, g_n, ALU.min, ALU.subtract).then_inc(gate_step, 1)
                    dve.wait_ge(gate_step, 3)
                    nc.vector.tensor_tensor_scan(g_B, ones[:], g_f, 0.0, ALU.mult, ALU.add).then_inc(gate_step, 1)
                    dve.wait_ge(gate_step, 4)
                    dve.wait_ge(iw_copied, 1)
                    nc.vector.scalar_tensor_tensor(rows_t[0:HEADS, :], rows[0:HEADS, :], gate_bias[0:HEADS, :], g_B,
                                                   ALU.add, ALU.subtract).then_inc(gate_step, 1)
                    dve.wait_ge(gate_step, 5)
                    nc.vector.tensor_tensor_scan(g_M, rows_t[0:HEADS, :], rows_t[0:HEADS, :], 0.0, ALU.max,
                                                 ALU.max).then_inc(gate_step, 1)
                    dve.wait_ge(gate_step, 6)
                    nc.vector.tensor_tensor(rows_t[32:32 + HEADS, :], g_B, g_M, ALU.add).then_inc(gate_step, 1)

                def index_sum(n):
                    j, h = n // HEADS + 1, n % HEADS
                    w = (j + 1) * P
                    acc = score[:, SCORE_AT[j]:SCORE_AT[j] + w]
                    dve.wait_ge(idx_relu, n + 1)
                    if h == 0:
                        dve.wait_ge(cols_done, 2)
                        ins = nc.vector.tensor_scalar(acc, relu_s[:, n % 2, :w], iw_col[:, j, h:h + 1], None, ALU.mult)
                    else:
                        dve.wait_ge(idx_acc, n)
                        ins = nc.vector.scalar_tensor_tensor(acc, relu_s[:, n % 2, :w], iw_col[:, j, h:h + 1], acc,
                                                             ALU.mult, ALU.add)
                    ins.then_inc(idx_acc, 1)

                ROUNDS = TOPK // 8
                STEPS = 2 * ROUNDS + 2

                def topk(r):
                    j, r = divmod(r, ROUNDS)
                    j += 1
                    sc = score[:, SCORE_AT[j]:SCORE_AT[j] + (j + 1) * P]
                    at = STEPS * (j - 1) + 2 * r
                    if r == 0:
                        dve.wait_ge(score_ready, j)
                    if at:
                        dve.wait_ge(tk, at)
                    nc.vector.max(top8[:], sc).then_inc(tk, 1)
                    dve.wait_ge(tk, at + 1)
                    nc.vector.match_replace(sc, top8[:], sc, TAKEN).then_inc(tk, 1)
                    if r == ROUNDS - 1:
                        dve.wait_ge(tk, at + 2)
                        nc.vector.tensor_scalar(sc, sc, TAKEN, None, ALU.is_equal).then_inc(tk, 1)
                        dve.wait_ge(tk, at + 3)
                        nc.vector.tensor_scalar(sc, sc, -MASKED, MASKED, ALU.mult, ALU.add).then_inc(tk, 1)

                def ml_probs(n):
                    w = (n // HEADS + 1) * P
                    dve.wait_ge(st_done, n + 1)
                    dve.wait_ge(decay_cut, n + 1)
                    if n >= 2:
                        dve.wait_ge(ml_pv, n - 1)
                    nc.vector.scalar_tensor_tensor(sbuf_pt[:, n % 2, :w], ps[:, 2 + n % 2, :w], DK ** -0.5,
                                                   sbuf_s[:, n % 2, :w], ALU.mult, ALU.mult).then_inc(ml_p, 1)

                def ml_divide(p):
                    j, a = p // 2, 2 * (p % 2)
                    o = ps[:, 6 + p % 2, 0:2 * (ML_DV + 1)].rearrange("p (h e) -> p h e", h=2)
                    y = Y[:, j, a * ML_DV:(a + 2) * ML_DV].rearrange("p (h e) -> p h e", h=2)
                    d, r = den[:, j, a:a + 2], rden[:, j, a:a + 2]
                    dve.wait_ge(ml_pv, 2 * (p + 1))
                    nc.vector.scalar_tensor_tensor(d, o[:, :, ML_DV], -1.0, expm[:, j, a:a + 2], ALU.mult,
                                                   ALU.max).then_inc(ml_step, 1)
                    dve.wait_ge(ml_step, 4 * p + 1)
                    nc.vector.tensor_tensor(d, o[:, :, ML_DV], d, ALU.max).then_inc(ml_step, 1)
                    dve.wait_ge(ml_step, 4 * p + 2)
                    nc.vector.reciprocal(r, d).then_inc(ml_step, 1)
                    dve.wait_ge(ml_step, 4 * p + 3)
                    nc.vector.tensor_tensor(y, o[:, :, 0:ML_DV], r[:, :, None].to_broadcast([P, 2, ML_DV]),
                                            ALU.mult).then_inc(ml_fin, 1)
                    dve.wait_ge(ml_fin, p + 1)
                    if p:
                        dve.wait_ge(hms_done, p)
                    nc.vector.tensor_tensor(sq[:].rearrange("p (h e) -> p h e", h=2), y, y, ALU.mult).then_inc(ml_step, 1)
                    dve.wait_ge(ml_step, 4 * p + 4)
                    nc.vector.tensor_reduce(hms[:, j, a:a + 2], sq[:].rearrange("p (h e) -> p h e", h=2), AX.X,
                                            ALU.add).then_inc(hms_done, 1)

                def ml_gated(j):
                    dve.wait_ge(hrstd_done, 2 * (j + 1))
                    dve.wait_ge(ml_gained, 2 * (j + 1))
                    dve.wait_ge(gate_done, j + 1)
                    for h in range(HEADS):
                        y = Y[:, j, h * ML_DV:(h + 1) * ML_DV]
                        ins = nc.vector.scalar_tensor_tensor(y, y, hrstd[:, j, h:h + 1],
                                                             ml_gate[:, j, h * ML_DV:(h + 1) * ML_DV], ALU.mult,
                                                             ALU.mult)
                    ins.then_inc(ml_out, 1)

                def sm_mask(m):
                    grp, j = divmod(m // HEADS, NT)
                    w = (j + 1) * P
                    dve.wait_ge(sc_done, m + 1)
                    if m >= 2:
                        dve.wait_ge(exp_done, m - 1)
                    if grp == 1 and j:
                        dve.wait_ge(tk, STEPS * j)
                    nc.vector.tensor_tensor_reduce(sbuf_s[:, m % 2, :w], ps[:, 2 + m % 2, :w], mask_of(grp, j),
                                                   -DK ** -0.5, 3e38, ALU.add, ALU.min,
                                                   nmin[:, m % 2:m % 2 + 1]).then_inc(sm_masked, 1)

                def sm_divide(k):
                    grp, j = divmod(k, NT)
                    dve.wait_ge(pv_done, HEADS * (k + 1))
                    nc.vector.reciprocal(rsum[:, k % 2], sums[:, k % 2]).then_inc(rsum_done, 1)
                    dve.wait_ge(rsum_done, k + 1)
                    c = W_V + grp * W_SM
                    nc.vector.tensor_tensor(Y[:, j, c:c + W_SM].rearrange("p (h e) -> p h e", h=HEADS),
                                            ps[:, 6 + k % 2, 0:W_SM].rearrange("p (h e) -> p h e", h=HEADS),
                                            rsum[:, k % 2][:, :, None].to_broadcast([P, HEADS, DK]),
                                            ALU.mult).then_inc(sm_fin, 1)

                def head_step(n):
                    if N_ML <= n < N_TASKS:
                        sm_mask(n - N_ML)
                    if 1 <= n <= N_ML:
                        ml_probs(n - 1)
                    if n % 2 == 0 and 4 <= n <= N_ML + 2:
                        ml_divide((n - 4) // 2)
                    if n % HEADS == 2 and n >= N_ML + 6:
                        sm_divide((n - N_ML - 6) // HEADS)
                    if n < 3 * ROUNDS - PARTS:
                        topk(n + PARTS)

                for j in range(IDX_FROM):
                    if j == 0:
                        dve.wait_ge(conv_t, 1)
                        nc.vector.tensor_copy(conv_w[:], ps[:, 4, 0:16]).then_inc(conv_w_ready, 1)
                    split_lo(j + 2)
                    if j == 2:
                        gates_f()
                        gates_scan()
                for j in range(IDX_FROM, N_PROJ):
                    for part in range(PARTS):
                        if (j, part) in CONV_AT:
                            conv(CONV_AT.index((j, part)))
                        if part == 0 and j > IDX_FROM:
                            if j + 1 == N_PROJ:
                                begin(dve, 1, l)
                            split_lo(j + 1)
                        if j < HEAD_FROM:
                            index_sum((j - IDX_FROM) * PARTS + part)
                            if j == HEAD_FROM - 1:
                                topk(part)
                        else:
                            head_step((j - HEAD_FROM) * PARTS + part)
                split_lo(N_PROJ + 1)
                ml_gated(0)
                ml_gated(1)

                for n in range(2 * NT):
                    c, i = divmod(n, NT)
                    if n in (1, 2):
                        ml_gated(n + 1)
                    if n == NT:
                        sm_divide(2 * NT - 1)
                    dve.wait_ge(nhi_done[0], 8 + n + 1)
                    nc.vector.tensor_tensor(
                        hT_lo[:, 4 * c:4 * c + 4, i * P:(i + 1) * P], ps[:, n, :].rearrange("p (k t) -> p k t", k=4),
                        hT_hi[:, 4 * c:4 * c + 4, i * P:(i + 1) * P].bitcast(F32), ALU.subtract).then_inc(nlo_done[0], 1)
                dve.sem_inc(part_over[0], 1)
                split_lo(N_PROJ + 2)
                split_lo(N_PROJ + 3)

                def mixed_gain(i):
                    dve.wait_ge(ms_done[1], NORM_AT[1, i])
                    gain_on(1, i, ps[:, 2 * i:2 * i + 2, :].rearrange("p a b -> p (a b)"), Y[:, i])

                def mixed(i):
                    apply(1, i, Y[:, i])

                for i in (0, 1):
                    mixed_gain(i)
                    mixed(i)
                normed(2, 0)
                normed(2, 1)
                split_lo(N_PRE)
                norm_lo(1, 0)
                mixed_gain(2)
                mixed(2)
                norm_lo(1, 1)
                dve.sem_inc(y_out, 8)
                dve.sem_inc(hid_ready, 2)
                mixed_gain(3)
                mixed(3)
                normed(2, 2)
                normed(2, 3)
                norm_lo(1, 2)
                norm_lo(1, 3)
                split_lo(N_PRE + 1)
                dve.wait_ge(y_zero, NT)

                def hidden(g, m):
                    dve.wait_ge(hid_ready, g * HID + m + 1)
                    dve.wait_ge(hid_relu, g * HID + m + 1)
                    nc.vector.tensor_tensor(hid_h[:, m % 2], hid_r[:, m % 2], hid_r[:, m % 2],
                                            ALU.mult).then_inc(hid_sq, 1)
                    dve.wait_ge(hid_hi_done, g * HID + m + 1)
                    dve.wait_ge(hid_sq, g * HID + m + 1)
                    nc.vector.tensor_tensor(hid_lo[:, m], hid_h[:, m % 2], hid_hi[:, m].bitcast(F32),
                                            ALU.subtract).then_inc(hid_ready, 1)

                def y_add(g, c, i):
                    dve.wait_ge(mm_done[1], mlp_event(g, 5 + 2 * c, i))
                    dve.wait_ge(y_out, g * 8 + (4 * c + i + 1))
                    y = Y[:, i, c * 512:(c + 1) * 512]
                    nc.vector.tensor_tensor(y, y, ps[:, 4 * c + i, :], ALU.add).then_inc(y_out, 1)

                def group(g, is_last):
                    for jj in range(GU):
                        if jj < 4:
                            hidden(g, 2 * jj)
                            hidden(g, 2 * jj + 1)
                        if jj + 2 < GU or not is_last:
                            split_lo_at(1, g * GU + (N_OUT + jj + 2), jj)
                        if jj == 5 or jj == 7 and not is_last:
                            for i in range(NT):
                                y_add(g, (jj - 5) // 2, i)

                with dve.Fori(0, GROUPS - 1) as g:
                    group(g, False)
                group(GROUPS - 1, True)
                dve.wait_ge(hid_ready, GROUPS * HID + 2)
                for i in range(NT):
                    y_add(GROUPS - 1, 1, i)
                    dve.wait_ge(y_out, 8 * GROUPS + 4 + i + 1)
                    if i >= 2:
                        dve.wait_ge(applied, NT + i - 1)
                    gain_on(3, i, Y[:, i], gained[i % 2])
                    if i:
                        apply(3, i - 1, gained[(i - 1) % 2])
                apply(3, NT - 1, gained[(NT - 1) % 2])
                dve.wait_ge(applied, 2 * NT)

        @block.tensor
        def _(pe):
            pe.wait_ge(const_step, 3)
            with pe.Fori(0, DEPTH) as l:
                begin(pe, 0, l)

                def turn(stage, i):
                    pe.wait_ge(xn_done[stage], i + 1)
                    if stage == 0:
                        pe.wait_ge(y_out, 8 * GROUPS + 2 * (i + 1))
                    for c in range(2):
                        for q in range(4):
                            k = 4 * c + q
                            ins = nc.tensor.transpose(ps[:, 2 * i + c, q * P:(q + 1) * P],
                                                      Y[:, i, k * P:(k + 1) * P], ident[:])
                        ins.then_inc(nt_done[stage], 1)

                def passes(o, st, mv, first, final):
                    nc.tensor.matmul(o, st[0], mv[1], start=first, stop=False)
                    nc.tensor.matmul(o, st[0], mv[0], start=False, stop=False)
                    return nc.tensor.matmul(o, st[1], mv[0], start=False, stop=final)

                def unit_part(j, part):
                    kind = UNITS[j][0]
                    hi, lo = slot(w_hi, j, "in"), slot(w_lo, j, "in")
                    n = tiles_of(j) * KD * 3 // PARTS
                    for at in range(part * n, (part + 1) * n):
                        t, k, which = at // (3 * KD), at // 3 % KD, at % 3
                        x = tiles_before(j) + t
                        if at == 0:
                            pe.wait_ge(lo_ready[0], j + 1)
                        if j == 0 and at % (3 * KD) == 0:
                            pe.wait_ge(nlo_done[0], 2 * (t + 1))
                        if at % (3 * KD) == 0 and x >= 2:
                            pe.wait_ge(tile_out, x - 1)
                        s = slice(t * P, (t + 1) * P)
                        first, final = at % (3 * KD) == 0, at % (3 * KD) == 3 * KD - 1
                        st_hi, st_lo = (hT_hi[:, k, s], hT_lo[:, k, s]) if kind == "t" else (hi[:, k, s], lo[:, k, s])
                        mv_hi, mv_lo = (hi[:, k, :], lo[:, k, :]) if kind == "t" else (hT_hi[:, k, :], hT_lo[:, k, :])
                        ins = nc.tensor.matmul(ps[:, x % 2, 0:256] if kind == "t" else ps[:, x % 2, :],
                                               st_lo if which == 2 else st_hi, mv_lo if which == 0 else mv_hi,
                                               start=first, stop=final)
                        if final:
                            ins.then_inc(mm_done[0], 1)

                def index_scores(n):
                    j, h = n // HEADS + 1, n % HEADS
                    if n == 0:
                        pe.wait_ge(tile_out, tiles_before(4))
                    if n >= 2:
                        pe.wait_ge(idx_relu, n - 1)
                    b = DK * (h % 2)
                    nc.tensor.matmul(ps[:, 2 + n % 2, :(j + 1) * P], ix_q[b:b + DK, h // 2, j * P:(j + 1) * P],
                                     ix_k[b:b + DK, :(j + 1) * P], start=True, stop=True).then_inc(idx_done, 1)

                def ml_spread(j):
                    if j == 0:
                        pe.wait_ge(cols_done, 3)
                    if j >= 2:
                        pe.wait_ge(decay_done, HEADS * (j - 1))
                    for h in range(HEADS):
                        ins = nc.tensor.matmul(ps[:, 4 + j % 2, h * P:(h + 1) * P], pick[:, h, :],
                                               g_M[:, j * P:(j + 1) * P], start=True, stop=True)
                    ins.then_inc(spread_done, 1)

                def ml_scores(n):
                    j, h = divmod(n, HEADS)
                    b = DK * (h % 2)
                    if n in (0, 2):
                        pe.wait_ge(silu_done, 3 + n // 2)
                    if n < 2:
                        pe.wait_ge(idx_relu, N_IDX)
                    else:
                        pe.wait_ge(ml_p, n - 1)
                    for i in range(j + 1):
                        ins = nc.tensor.matmul(ps[:, 2 + n % 2, i * P:(i + 1) * P],
                                               ml_qk[b:b + DK, 2 + h // 2, i * P:(i + 1) * P],
                                               ml_qk[b:b + DK, h // 2, j * P:(j + 1) * P], start=True, stop=True)
                    ins.then_inc(st_done, 1)

                def ml_values(n):
                    j, h = divmod(n, HEADS)
                    p = n // 2
                    pe.wait_ge(ml_p, n + 1)
                    if n == 0:
                        pe.wait_ge(tile_out, tiles_before(HEAD_FROM))
                    if n % 2 == 0 and p >= 2:
                        pe.wait_ge(ml_fin, p - 1)
                    c = (ML_DV + 1) * (n % 2)
                    for i in range(j + 1):
                        ins = nc.tensor.matmul(ps[:, 6 + p % 2, c:c + ML_DV + 1],
                                               sbuf_pt[:, n % 2, i * P:(i + 1) * P], ml_v[:, i, h, :],
                                               start=(i == 0), stop=(i == j))
                    ins.then_inc(ml_pv, 1)

                def sm_scores(m):
                    k, h = divmod(m, HEADS)
                    grp, j = divmod(k, NT)
                    b = DK * (h % 2)
                    if m % N_ML == 0:
                        pe.wait_ge(tile_out, tiles_before(8 if grp == 0 else 11))
                    if m < 2:
                        pe.wait_ge(ml_p, N_ML - 1 + m)
                    else:
                        pe.wait_ge(sm_masked, m - 1)
                    nc.tensor.matmul(ps[:, 2 + m % 2, :(j + 1) * P], sm_qk[grp][b:b + DK, h // 2, j * P:(j + 1) * P],
                                     sm_qk[grp][b:b + DK, 2 + h // 2, :(j + 1) * P], start=True,
                                     stop=True).then_inc(sc_done, 1)

                def sm_turn(m):
                    j = m // HEADS % NT
                    pe.wait_ge(exp_done, m + 1)
                    if m < 2:
                        pe.wait_ge(decay_done, N_ML)
                    else:
                        pe.wait_ge(pt_out, m - 1)
                    for i in range(j + 1):
                        ins = nc.tensor.transpose(ps[:, 4 + m % 2, i * P:(i + 1) * P],
                                                  sbuf_p[:, m % 2, i * P:(i + 1) * P], ident[:])
                    ins.then_inc(pt_done, 1)

                def sm_values(m):
                    k, h = divmod(m, HEADS)
                    grp, j = divmod(k, NT)
                    pe.wait_ge(pt_out, m + 1)
                    if h == 0:
                        pe.wait_ge(tile_out, tiles_before(8 if grp == 0 else 11) + j + 1)
                        if k < 2:
                            pe.wait_ge(ml_fin, N_ML // 2 - 1 + k)
                        else:
                            pe.wait_ge(sm_fin, k - 1)
                    for i in range(j + 1):
                        ins = nc.tensor.matmul(ps[:, 6 + k % 2, h * DK:(h + 1) * DK],
                                               sbuf_pt[:, m % 2, i * P:(i + 1) * P],
                                               sm_v[:, i, HEADS * grp + h, :], start=(i == 0), stop=(i == j))
                    ins.then_inc(pv_done, 1)

                def head_step(n):
                    if n < N_ML:
                        if n % HEADS == 0:
                            ml_spread(n // HEADS)
                        ml_scores(n)
                    elif n < N_TASKS:
                        sm_scores(n - N_ML)
                    if N_ML < n <= N_TASKS:
                        sm_turn(n - 1 - N_ML)
                    if 2 <= n < N_ML + 2:
                        ml_values(n - 2)
                    elif n >= N_ML + 2:
                        sm_values(n - 2 - N_ML)

                pe.wait_ge(y_out, 8 * GROUPS + 4)
                for _ in range(WARM):
                    nc.tensor.transpose(ps[:, 3, 0:P], ident[:], ident[:])
                turn(0, 0)
                turn(0, 1)
                pe.wait_ge(const_step, 10)
                for j in range(IDX_FROM):
                    for part in range(PARTS):
                        unit_part(j, part)
                        if j == 0 and part in (1, 2):
                            turn(0, 1 + part)
                    if j == 0:
                        pe.wait_ge(mm_done[1], LATE_EVENTS)
                        pe.sem_inc(part_over[1], 1)
                        pe.wait_ge(params_loaded, 64)
                        pe.wait_ge(nlo_done[0], 8)
                        nc.tensor.transpose(ps[:, 4, 0:16], conv_rows[:], ident[0:16, 0:16]).then_inc(conv_t, 1)

                def turn_rows():
                    pe.wait_ge(gate_step, 7)
                    pe.wait_ge(iw_copied, 1)
                    pe.wait_ge(conv_w_ready, 1)
                    for t in range(NT):
                        ins = nc.tensor.transpose(ps[:, 4, t * 36:(t + 1) * 36],
                                                  rows_t[0:36, t * P:(t + 1) * P], ident[0:36, 0:36])
                    ins.then_inc(rows_turned, 1)

                for j in range(IDX_FROM, N_PROJ):
                    for part in range(PARTS):
                        unit_part(j, part)
                        if j < HEAD_FROM:
                            index_scores((j - IDX_FROM) * PARTS + part)
                            if (j, part) == (IDX_FROM, 1):
                                turn_rows()
                        else:
                            head_step((j - HEAD_FROM) * PARTS + part)

                def mix_turn(n):
                    c, i = divmod(n, NT)
                    for q in range(4):
                        k = 4 * c + q
                        ins = nc.tensor.transpose(ps[:, n, q * P:(q + 1) * P], Y[:, i, k * P:(k + 1) * P], ident[:])
                    ins.then_inc(nt_done[0], 1)

                def out_tile(j, t):
                    pe.wait_ge(lo_ready[1], j + 1 - N_PROJ)
                    hi, lo = slot(w_hi, j, "out"), slot(w_lo, j, "out")
                    s = slice(t * P, (t + 1) * P)
                    for c in range(2):
                        for k in range(2):
                            kk = 2 * (j - N_PROJ) + k
                            cs = slice(c * 512, (c + 1) * 512)
                            ins = passes(ps[:, 2 * t + c, :], (hT_hi[:, kk, s], hT_lo[:, kk, s]),
                                         (hi[:, k, cs], lo[:, k, cs]), kk == 0, kk == KD - 1)
                    ins.then_inc(mm_done[1], 1)

                head_step(N_TASKS)
                pe.wait_ge(tile_out, PROJ_TILES)
                pe.wait_ge(sm_masked, N_SM)
                begin(pe, 1, l)
                order = iter(OUT_ORDER)

                def out_next(n):
                    for _ in range(n):
                        j, t = next(order)
                        out_tile(N_PROJ + j, t)

                for i in range(NT):
                    pe.wait_ge(ml_out, i + 1)
                    mix_turn(i)
                    if i == 1:
                        head_step(N_TASKS + 1)
                    if i >= 2:
                        pe.wait_ge(nlo_done[0], 8 + 2)
                        out_next(1)
                pe.wait_ge(nlo_done[0], 8 + NT)
                out_next(2)
                pe.wait_ge(pt_out, N_SM)
                for i in range(NT):
                    pe.wait_ge(sm_fin, NT + i + (2 if i == 2 else 1))
                    mix_turn(NT + i)
                pe.wait_ge(nlo_done[0], 8 + NT + 2)
                out_next(1)
                pe.wait_ge(nlo_done[0], 8 + 2 * NT)
                out_next(1)
                pe.sem_inc(part_over[0], 1)
                out_next(8)
                turn(1, 0)
                out_next(1)
                turn(1, 1)
                out_next(1)

                def ff1_tile(jj, t, cols, m):
                    hi, lo = slot(w_hi, jj, "in"), slot(w_lo, jj, "in")
                    s = slice(t * P, (t + 1) * P)
                    for k in range(KD):
                        ins = passes(ps[:, m, cols], (hi[:, k, s], lo[:, k, s]),
                                     (hT_hi[:, k, cols], hT_lo[:, k, cols]), k == 0, k == KD - 1)
                    return ins

                def ff1_unit(g, jj):
                    pe.wait_ge(lo_ready[1], g * GU + (N_OUT + jj + 1))
                    for t in range(2):
                        m = 2 * jj + t
                        pe.wait_ge(y_out, g * 8 + m + 1)
                        ff1_tile(jj, t, slice(0, SEQ), m).then_inc(mm_done[1], 1)

                def ff2_unit(g, jj):
                    c, kh = (jj - 4) // 2, jj % 2
                    hi, lo = slot(w_hi, jj, "t"), slot(w_lo, jj, "t")
                    pe.wait_ge(lo_ready[1], g * GU + (N_OUT + jj + 1))
                    if jj < 6:
                        pe.wait_ge(hid_ready, g * HID + (4 * kh + 4 + 2))
                    for t in range(NT):
                        s = slice(t * P, (t + 1) * P)
                        for k in range(4):
                            kk = 4 * kh + k
                            ins = passes(ps[:, 4 * c + t, :], (hid_hi[:, kk, s], hid_lo[:, kk, s]),
                                         (hi[:, k, :], lo[:, k, :]), kk == 0, kk == HID - 1)
                        ins.then_inc(mm_done[1], 1)

                def group(g, is_last):
                    for jj in range(1, GU):
                        if jj < 4:
                            ff1_unit(g, jj)
                        else:
                            ff2_unit(g, jj)
                    if not is_last:
                        ff1_unit(g + 1, 0)

                pe.wait_ge(lo_ready[1], N_OUT + 1)
                pe.wait_ge(y_out, 2)
                pe.wait_ge(nlo_done[1], 4)
                for t in range(2):
                    ff1_tile(0, t, slice(0, 2 * P), t)
                turn(1, 2)
                turn(1, 3)
                pe.wait_ge(nlo_done[1], 8)
                for t in range(2):
                    ff1_tile(0, t, slice(2 * P, 4 * P), t).then_inc(mm_done[1], 1)
                with pe.Fori(0, GROUPS - 1) as g:
                    group(g, False)
                group(GROUPS - 1, True)


_INS = ["x", "norm_mix_pre", "w_in", "ml_conv", "ml_i_bias", "ml_f_bias", "ml_head_norm", "w_out",
        "norm_mix_post", "norm_mlp_pre", "w_ff1", "w_ff2", "norm_mlp_post"]


def kernel(**inputs):
    import numpy as np
    import concourse.bacc as bacc
    from concourse.bass_utils import run_bass_kernel_spmd

    nc = bacc.Bacc("TRN2", target_bir_lowering=False, num_devices=1)
    arrays, args = {}, []
    for name in _INS:
        a = np.ascontiguousarray(inputs[name])
        arrays[f"in_{name}"] = a
        args.append(nc.dram_tensor(f"in_{name}", a.shape, mybir.dt.from_np(a.dtype), kind="ExternalInput").ap())
    shape = (1, SEQ, D)
    args.append(nc.dram_tensor("out_x", shape, F32, kind="ExternalOutput").ap())
    trunk(nc, *args)
    r = run_bass_kernel_spmd(nc, [arrays], core_ids=[0])
    return r.results[0]["out_x"]
```

```python
from contextlib import ExitStack

import concourse.bass as bass
from concourse import mybir

F32 = mybir.dt.float32
F32R = mybir.dt.float32r
ALU = mybir.AluOpType
ACT = mybir.ActivationFunctionType
AX = mybir.AxisListType

P = 128
DEPTH, SEQ, D = 2, 512, 1024
NT = SEQ // P
KD = D // P
HEADS, DK, ML_DV = 4, 64, 128
TOPK = min(256, SEQ // 4)
D_FF = 4 * D
EPS = 1e-6
W_QK, W_V, W_SM = HEADS * DK, HEADS * ML_DV, HEADS * DK
(C_MLQ, C_MLK, C_MLV, C_MLO, C_I, C_F, C_MBQ, C_MBK, C_MBV, C_DSQ, C_DSK, C_DSV, C_IXQ, C_IXK, C_IXW) = (
    0, 256, 512, 1024, 1536, 1540, 1544, 1800, 2056, 2312, 2568, 2824, 3080, 3336, 3400)

UNIT = 2048
UNITS = [("t", C_MLV), ("t", C_MLV + 256), ("small", None), ("f", C_IXQ), ("f", C_MLK), ("f", C_MLQ),
         ("f", C_MBQ), ("f", C_MBK), ("t", C_MBV), ("f", C_DSQ), ("f", C_DSK), ("t", C_DSV),
         ("t", C_MLO), ("t", C_MLO + 256)]
N_PROJ = len(UNITS)
N_OUT = 4
N_PRE = N_PROJ + N_OUT
GROUPS = 4
HID = D_FF // GROUPS // P
GU = 8

PARTS = 6
IDX_FROM = 4
HEAD_FROM = 6
CONV_CHUNK = (2, 3, 0, 1)
CONV_AT = [(4, 4), (5, 0), (5, 3), (5, 5)]
SILU_AT = [(5, 0), (5, 1), (5, 4), (6, 0)]
WARM = 60
N_IDX = (NT - 1) * HEADS
N_ML = NT * HEADS
N_SM = 2 * NT * HEADS
N_TASKS = N_ML + N_SM
assert (HEAD_FROM - IDX_FROM) * PARTS == N_IDX and (N_PROJ - HEAD_FROM) * PARTS == N_TASKS
AHEAD = 4
TAIL = 2


def steps_of(j, part):
    at = (j - HEAD_FROM) * PARTS + part
    return [at] if at < 2 else [2 * at - 2, 2 * at - 1] if at < 2 + TAIL else [at + TAIL]


MASKED = -1e30
ABSENT, TAKEN = -2e38, -3e38
SCORE_AT = {j: P * sum(i + 1 for i in range(1, j)) for j in range(1, NT)}
SCORE_SIZE = SCORE_AT[NT - 1] + SEQ

NORMS = ([(0, i) for i in range(NT)],
         [(1, 0), (1, 1), (2, 0), (2, 1), (1, 2), (1, 3), (2, 2), (2, 3)] + [(3, i) for i in range(NT)])
NORM_PART = {k: part for part in (0, 1) for k in NORMS[part]}
NORM_AT = {k: n + 1 for part in (0, 1) for n, k in enumerate(NORMS[part])}


def tiles_of(j):
    return {"t": 4, "f": 2, "small": 1}[UNITS[j][0]] if j < N_PROJ else 4


def tiles_before(j):
    return sum(tiles_of(i) for i in range(j))


PROJ_TILES = tiles_before(N_PROJ)


def tiles_in_part(j, part):
    n = tiles_of(j)
    return range(part * n // PARTS, (part + 1) * n // PARTS)


N_LATE = N_OUT + GROUPS * GU
GROUP_EVENTS = 4 * 2 + 4 * 4
EV_MLP = N_OUT * NT
LATE_EVENTS = EV_MLP + GROUPS * GROUP_EVENTS


def mlp_event(g, jj, t):
    before = 2 * jj if jj < 4 else 8 + 4 * (jj - 4)
    return g * GROUP_EVENTS + (EV_MLP + before + t + 1)


def unit_end(g, jj):
    if jj >= 0:
        return mlp_event(g, jj, 1 if jj < 4 else 3)
    return g * GROUP_EVENTS + (EV_MLP + 4 * (jj + 1))


def dmas_of(j):
    return 4 if UNITS[j][0] == "small" else 1


def raw_landed(j):
    if j >= N_PROJ:
        return 16 * ((j - N_PROJ) // 2 + 1)
    return 16 * sum(dmas_of(i) for i in range(j % 2, j + 1, 2))


OUT_ORDER = [(0, 0), (0, 1), (0, 2), (0, 3), (1, 0), (1, 1), (1, 2), (1, 3),
             (2, 0), (2, 1), (3, 0), (3, 1), (2, 2), (2, 3), (3, 2), (3, 3)]


TURNS = (0, 1, 4, 5, 2, 3, 6, 7)


def out_event(j, t):
    return OUT_ORDER.index((j, t)) + 1


def out_unit_end(j):
    return max(out_event(j, t) for t in range(NT))


RAW_OUT = 16 * N_OUT // 2


def trunk(nc, x, norm_mix_pre, w_in, ml_conv, ml_i_bias, ml_f_bias, ml_head_norm, w_out,
          norm_mix_post, norm_mlp_pre, w_ff1, w_ff2, norm_mlp_post, out):
    ctx = ExitStack()
    with ctx:
        def sb(name, shape, dt=F32, on=ctx):
            return on.enter_context(nc.sbuf_tensor(name, shape, dt))

        m_rows = nc.dram_tensor("m_rows", (HEADS, SEQ), F32, kind="Internal").ap()
        X = sb("X", [P, NT, D])
        Y = sb("Y", [P, NT, D])
        gain_pre = sb("gain_pre", [P, D])
        gain_post = sb("gain_post", [P, D])
        head_gain = sb("head_gain", [P, W_V])
        raw = sb("raw", [P, 2, UNIT])
        w_hi = sb("w_hi", [P, 2, UNIT], F32R)
        w_lo = sb("w_lo", [P, 2, UNIT], F32R)
        hT_hi = sb("hT_hi", [P, KD, SEQ], F32R)
        hT_lo = sb("hT_lo", [P, KD, SEQ], F32R)
        sbuf_s = sb("scores", [P, 2, SEQ])
        sbuf_p = sb("probs", [P, 2, SEQ])
        sbuf_pt = sb("probs_t", [P, 2, SEQ])
        sq = sb("squares", [P, 2 * ML_DV])
        with ExitStack() as shared:
            hid_hi = sb("hid_hi", [P, HID, SEQ], F32R, shared)
            hid_lo = sb("hid_lo", [P, HID, SEQ], F32R, shared)
            hid_r = sb("hid_r", [P, 2, SEQ], on=shared)
            hid_h = sb("hid_h", [P, 2, SEQ], on=shared)
        ml_qk = sb("ml_qk", [P, 4, SEQ])
        sm_qk = [sb("mb_qk", [P, 4, SEQ]), sb("ds_qk", [P, 4, SEQ])]
        ix_q = sb("ix_q", [P, 2, SEQ])
        ix_k = sb("ix_k", [P, SEQ])
        ml_gate = sb("ml_gate", [P, NT, W_V])
        sb("unused", [P, (2 * HID + 4) * SEQ - 15 * SEQ - NT * W_V])
        rows_t = sb("rows_t", [P, SEQ])
        ml_v = sb("ml_v", [P, NT, HEADS, ML_DV + 1])
        sm_v = sb("sm_v", [P, NT, 2 * HEADS, DK])
        score = sb("score", [P, SCORE_SIZE])
        causal = sb("causal", [P, SEQ])
        ones = sb("ones", [HEADS, SEQ])
        ident = sb("ident", [P, P])
        half = sb("half", [P, HEADS])
        conv_rows = sb("conv_rows", [16, P])
        conv_w = sb("conv_w", [P, 16])
        gate_bias = sb("gate_bias", [P, 1])
        a_col = sb("a_col", [P, NT, HEADS])
        a_neg = sb("a_neg", [P, NT, HEADS])
        expm = sb("expm", [P, NT, HEADS])
        iw_col = sb("iw_col", [P, NT, HEADS])
        ms = sb("ms", [P, 16])
        ms_eps = sb("ms_eps", [P, 16])
        rstd = sb("rstd", [P, 16])
        hms = sb("hms", [P, NT, HEADS])
        hms_eps = sb("hms_eps", [P, NT, HEADS])
        hrstd = sb("hrstd", [P, NT, HEADS])
        den = sb("den", [P, NT, HEADS])
        rden = sb("rden", [P, NT, HEADS])
        table_sink = sb("table_sink", [P, 1])
        top8 = sb("top8", [P, 8])
        nmin = sb("nmin", [P, 2])
        sums = sb("sums", [P, 2, HEADS])
        rsum = sb("rsum", [P, 2, HEADS])
        sq_sink = sb("sq_sink", [P, D], mybir.dt.bfloat16)
        rows = sbuf_pt[:, 0, :]
        relu_s = sbuf_p
        gained = [t[:].rearrange("p a b -> p (a b)") for t in (hid_r, hid_h)]
        conv_in = Y[:, 0, :].rearrange("p (b t) -> p b t", b=2)
        conv_acc = Y[:, 1, :].rearrange("p (b t) -> p b t", b=2)
        g_f, g_n = Y[0:HEADS, 2, 0:SEQ], Y[0:HEADS, 2, SEQ:2 * SEQ]
        g_B, g_M = Y[0:HEADS, 3, 0:SEQ], rows_t[64:64 + HEADS, :]
        m_all = Y[:, 2:4, :].rearrange("p a (b h t) -> p (a b) h t", b=2, h=HEADS)

        ps = ctx.enter_context(nc.psum_tensor("ps", [P, 8, 512], F32))

        early, late, standing = [], [], []

        def sem(name, of):
            h = ctx.enter_context(nc.semaphore(name))
            of.append(h.num)
            return h

        x_loaded = [sem(f"x{i}_loaded", standing) for i in range(NT)]
        stored = sem("stored", standing)
        table_loaded = sem("table_loaded", standing)
        const_step = sem("const_step", standing)
        part_go = [sem("early_go", standing), sem("late_go", standing)]
        part_begun = sem("part_begun", standing)

        def common(part, of):
            return {n: sem(f"{n}_{part}", of) for n in (
                "part_over", "raw0_loaded", "raw1_loaded", "gain_pre_loaded", "hi_ready", "lo_ready", "mm_done",
                "ms_done", "eps_done", "rstd_done", "xn_done", "nt_done", "nhi_done", "nlo_done")}

        first = common("early", early)
        params_loaded = sem("params_loaded", early)
        conv_t = sem("conv_t", early)
        conv_w_ready = sem("conv_w_ready", early)
        tile_out = sem("tile_out", early)
        conv_step = sem("conv_step", early)
        silu_done = sem("silu_done", early)
        gate_step = sem("gate_step", early)
        softplus_done = sem("softplus_done", early)
        iw_copied = sem("iw_copied", early)
        rows_turned = sem("rows_turned", early)
        cols_done = sem("cols_done", early)
        idx_done = sem("idx_done", early)
        idx_relu = sem("idx_relu", early)
        idx_acc = sem("idx_acc", early)
        score_ready = sem("score_ready", early)
        tk = sem("topk_step", early)
        m_stored = sem("m_stored", early)
        m_spread = sem("m_spread", early)
        st_done = sem("st_done", early)
        decay_arg = sem("decay_arg", early)
        decay_done = sem("decay_done", early)
        decay_cut = sem("decay_cut", early)
        ml_p = sem("ml_p", early)
        ml_pv = sem("ml_pv", early)
        ml_step = sem("ml_step", early)
        ml_fin = sem("ml_fin", early)
        hms_done = sem("hms_done", early)
        hms_eps_done = sem("hms_eps_done", early)
        hrstd_done = sem("hrstd_done", early)
        ml_gained = sem("ml_gained", early)
        gate_done = sem("gate_done", early)
        ml_out = sem("ml_out", early)
        sc_done = sem("sc_done", early)
        sm_masked = sem("sm_masked", early)
        exp_done = sem("exp_done", early)
        pt_done = sem("pt_done", early)
        pt_out = sem("pt_out", early)
        pv_done = sem("pv_done", early)
        rsum_done = sem("rsum_done", early)
        sm_fin = sem("sm_fin", early)
        second = common("late", late)
        gain_post_loaded = sem("gain_post_loaded", late)
        table_back = sem("table_back", late)
        half_ready_out = sem("half_ready_out", late)
        half_ready_mlp = sem("half_ready_mlp", late)
        applied_t = sem("applied_t", late)
        applied = sem("applied", late)
        hid_relu = sem("hid_relu", late)
        hid_sq = sem("hid_sq", late)
        hid_hi_done = sem("hid_hi_done", late)
        hid_ready = sem("hid_ready", late)
        y_zero = sem("y_zero", late)
        y_out = sem("y_out", late)
        assert late == list(range(late[0], late[-1] + 1)) and early == list(range(early[0], early[-1] + 1))
        part_over, gain_pre_loaded, hi_ready, lo_ready, mm_done, ms_done, eps_done, rstd_done, xn_done = (
            [of[n] for of in (first, second)] for n in (
                "part_over", "gain_pre_loaded", "hi_ready", "lo_ready", "mm_done", "ms_done", "eps_done",
                "rstd_done", "xn_done"))
        nt_done, nhi_done, nlo_done = ([of[n] for of in (first, second)] for n in ("nt_done", "nhi_done", "nlo_done"))
        raw_loaded = [[of["raw0_loaded"], of["raw1_loaded"]] for of in (first, second)]

        SLOTW = {"in": (8, 256), "t": (4, 512), "out": (2, 1024)}

        def slot(t, j, form):
            k, n = SLOTW[form]
            return t[:, j % 2, :].rearrange("p (k n) -> p k n", k=k)

        def mask_of(grp, j):
            n = (j + 1) * P
            if grp == 0 or j == 0:
                return causal[:, SEQ - n:SEQ]
            return score[:, SCORE_AT[j]:SCORE_AT[j] + n]

        def begin(eng, part, l):
            eng.wait_ge(part_go[part], l + 1)
            eng.sem_inc(part_begun, 1)
            eng.wait_ge(part_go[part], 1)

        block = ctx.enter_context(nc.Block())

        @block.sync
        def _(sp):
            sp.dma_start(X[:, 0], x[0, 0:P]).then_inc(x_loaded[0], 16)

            with sp.Fori(0, DEPTH) as l:
                begin(sp, 0, l)

                def load(dst, src, s):
                    sp.dma_start(dst, src).then_inc(s, 16)

                def load_unit(j):
                    s = raw_loaded[j >= N_PROJ][j % 2]
                    if j < 2:
                        sp.wait_ge(lo_ready[1], N_LATE - 1 + j)
                    elif j < N_PROJ + 2:
                        sp.wait_ge(lo_ready[0], j - 1)
                    else:
                        sp.wait_ge(lo_ready[1], j - 1 - N_PROJ)
                    if j >= N_PROJ:
                        r = (j - N_PROJ) * 2 * P
                        load(slot(raw, j, "out"), w_out[l, r:r + 2 * P, :].rearrange("(k p) n -> p k n", p=P), s)
                        return
                    w = w_in[l].rearrange("(k p) n -> p k n", p=P)
                    u = UNITS[j]
                    if u[0] != "small":
                        load(slot(raw, j, "in"), w[:, :, u[1]:u[1] + 256], s)
                    else:
                        d = slot(raw, j, "in")
                        for at, c, n in ((0, C_IXK, DK), (DK, C_I, HEADS), (DK + HEADS, C_IXW, HEADS),
                                         (DK + 32, C_F, HEADS)):
                            load(d[:, :, at:at + n], w[:, :, c:c + n], s)

                sp.wait_ge(xn_done[1], NT)
                load(gain_pre[:], norm_mix_pre[l][None, :].to_broadcast([P, D]), gain_pre_loaded[0])
                load_unit(0)
                sp.wait_ge(x_loaded[2], 16)
                load_unit(1)
                load(conv_rows[:], ml_conv[l].rearrange("k (c p) -> (k c) p", p=P), params_loaded)
                load(gate_bias[0:HEADS, :], ml_i_bias[l][:, None], params_loaded)
                load(gate_bias[32:32 + HEADS, :], ml_f_bias[l][:, None], params_loaded)
                load(head_gain[:], ml_head_norm[l][None, :].to_broadcast([P, W_V]), params_loaded)
                for j in range(2, N_PRE):
                    if j == 4:
                        sp.wait_ge(applied, 2 * NT)
                        sp.sem_inc(part_over[1], 1)
                        begin(sp, 1, l)
                        load(gain_post[:], norm_mix_post[l][None, :].to_broadcast([P, D]), gain_post_loaded)
                        sp.wait_ge(xn_done[0], NT)
                        load(gain_pre[:], norm_mlp_pre[l][None, :].to_broadcast([P, D]), gain_pre_loaded[1])
                    if j == 7:
                        sp.wait_ge(gate_step, 7)
                        load(m_rows[:], g_M, m_stored)
                        sp.wait_ge(m_stored, 16)
                        for h in range(HEADS):
                            load(m_all[:, :, h, :], m_rows[h:h + 1, :].rearrange("o (j t) -> o j t", j=NT)
                                 .to_broadcast([P, NT, P]), m_spread)
                    load_unit(j)
                    if j == N_PROJ + 1:
                        sp.sem_inc(part_over[0], 1)
                with sp.Fori(0, GROUPS) as g:
                    for jj in range(GU):
                        sp.wait_ge(lo_ready[1], g * GU + (N_OUT + jj - 1))
                        sp.wait_ge(x_loaded[0], 16)
                        if jj < 4:
                            src = w_ff1[l].rearrange("(k p) n -> p k n", p=P)[
                                :, :, bass.ds(g * (HID * P) + jj * 256, 256)]
                            load(slot(raw, jj, "in"), src, raw_loaded[1][jj % 2])
                        else:
                            c, half_k = (jj - 4) // 2, jj % 2
                            src = w_ff2[l, bass.ds(g * (HID * P) + half_k * 4 * P, 4 * P), c * 512:(c + 1) * 512]
                            load(slot(raw, jj, "t"), src.rearrange("(k p) n -> p k n", p=P), raw_loaded[1][jj % 2])
                sp.wait_ge(applied, NT)
                load(gain_post[:], norm_mlp_post[l][None, :].to_broadcast([P, D]), gain_post_loaded)
                sp.wait_ge(gain_post_loaded, 32)
            for i in range(NT):
                sp.wait_ge(applied, NT + i + 1)
                sp.dma_start(out[0, i * P:(i + 1) * P], X[:, i]).then_inc(stored, 16)
            sp.wait_ge(stored, 16 * NT)

        def head_pair(pool, p):
            j, a = p // 2, 2 * (p % 2)
            y = Y[:, j, a * ML_DV:(a + 2) * ML_DV]
            pool.wait_ge(hms_done, p + 1)
            nc.gpsimd.tensor_scalar(hms_eps[:, j, a:a + 2], hms[:, j, a:a + 2], 1.0 / ML_DV, EPS, ALU.mult,
                                    ALU.add).then_inc(hms_eps_done, 1)
            nc.gpsimd.tensor_tensor(y, y, head_gain[:, a * ML_DV:(a + 2) * ML_DV], ALU.mult).then_inc(ml_gained, 1)
            pool.wait_ge(hms_eps_done, p + 1)
            nc.gpsimd.tensor_tensor(hrstd[:, j, a:a + 2], hms_eps[:, j, a:a + 2], half[:, 0:2],
                                    ALU.pow).then_inc(hrstd_done, 1)

        @block.gpsimd
        def _(pool):
            steps = [0]

            def step(ins):
                steps[0] += 1
                ins.then_inc(const_step, 1)
                pool.wait_ge(const_step, steps[0])

            step(pool.memset(half[:], -0.5))
            for s, n in ((lo_ready[1], N_LATE), (xn_done[1], NT), (applied, 2 * NT), (mm_done[1], LATE_EVENTS),
                         (y_out, 8 * GROUPS + 8)):
                pool.sem_inc(s, n)
            pool.sem_inc(part_go[0], 1)
            step(pool.memset(ident[:], 0.0))
            step(pool.affine_select(out=ident[:], in_=ident[:], compare_op=ALU.not_equal, fill=1.0, base=0,
                                    pattern=[[-1, P]], channel_multiplier=1))
            step(pool.memset(causal[:], 0.0))
            step(pool.affine_select(out=causal[:, SEQ - P:SEQ], in_=causal[:, SEQ - P:SEQ], compare_op=ALU.is_ge,
                                    fill=MASKED, base=0, pattern=[[-1, P]], channel_multiplier=1))
            step(pool.memset(ones[:], 1.0))
            step(pool.memset(rows_t[:], 0.0))
            step(pool.memset(ml_v[:], 1.0))

            with pool.Fori(0, DEPTH) as l:
                def make_rstd(norm, i):
                    n, part = NORM_AT[norm, i], NORM_PART[norm, i]
                    c = slice(NT * norm + i, NT * norm + i + 1)
                    pool.wait_ge(ms_done[part], n)
                    nc.gpsimd.tensor_scalar(ms_eps[:, c], ms[:, c], EPS, None, ALU.add).then_inc(eps_done[part], 1)
                    pool.wait_ge(eps_done[part], n)
                    nc.gpsimd.tensor_tensor(rstd[:, c], ms_eps[:, c], half[:, 0:1],
                                            ALU.pow).then_inc(rstd_done[part], 1)

                def half_lo(j, half_of, half_done):
                    h = slice(half_of * UNIT // 2, (half_of + 1) * UNIT // 2)
                    pool.wait_ge(hi_ready[1], j + 1 - N_PROJ)
                    nc.gpsimd.tensor_tensor(w_lo[:, j % 2, h], raw[:, j % 2, h], w_hi[:, j % 2, h].bitcast(F32),
                                            ALU.subtract).then_inc(lo_ready[1] if half_of else half_done, 1)

                for norm, i in NORMS[0]:
                    make_rstd(norm, i)
                pool.wait_ge(part_over[1], 4)
                pool.sem_clear(range(late[0], late[-1] + 1))
                pool.sem_inc(part_go[1], 1)
                for j in range(1, NT):
                    pool.wait_ge(idx_acc, HEADS * j)
                    d = score[:, SCORE_AT[j] + j * P:SCORE_AT[j] + (j + 1) * P]
                    nc.gpsimd.affine_select(out=d, in_=d, compare_op=ALU.is_ge, fill=ABSENT, base=0,
                                            pattern=[[-1, P]], channel_multiplier=1).then_inc(score_ready, 1)
                pool.wait_ge(params_loaded, 64)
                for n in range(N_ML):
                    j = n // HEADS
                    pool.wait_ge(decay_done, n + 1)
                    d = sbuf_s[:, n % 2, j * P:(j + 1) * P]
                    nc.gpsimd.affine_select(out=d, in_=d, compare_op=ALU.is_ge, fill=0.0, base=0,
                                            pattern=[[1, P]], channel_multiplier=-1).then_inc(decay_cut, 1)
                    if n >= 5 and n % 2:
                        head_pair(pool, (n - 5) // 2)
                for p in range(N_ML // 2 - 2, N_ML // 2):
                    head_pair(pool, p)
                begin(pool, 1, l)
                for half_of in (0, 1):
                    half_lo(N_PROJ + 1, half_of, half_ready_out)
                pool.wait_ge(part_over[0], 4)
                pool.sem_clear(range(early[0], early[-1] + 1))
                pool.sem_inc(part_go[0], 1)
                for norm, i in NORMS[1]:
                    if norm == 1 and i >= 2:
                        half_lo(N_PRE, i - 2, half_ready_mlp)
                    if (norm, i) == (3, 0):
                        pool.wait_ge(nt_done[1], 8)
                        for t in range(NT):
                            nc.gpsimd.memset(Y[:, t], 0.0).then_inc(y_zero, 1)
                    make_rstd(norm, i)
                pool.wait_ge(rstd_done[1], len(NORMS[1]))

        @block.scalar
        def _(act):
            act.wait_ge(const_step, 1)
            nc.scalar.activation(sq_sink[:, 0:1], half[:, 0:1], ACT.Square).then_inc(table_loaded, 1)
            act.wait_ge(table_loaded, 1)
            act.wait_ge(x_loaded[0], 16)
            for i in range(1, NT):
                act.dma_start(X[:, i], x[0, i * P:(i + 1) * P]).then_inc(x_loaded[i], 16)
            with act.Fori(0, DEPTH) as l:
                begin(act, 0, l)

                def mean_square(norm, i, src):
                    n, part = NORM_AT[norm, i], NORM_PART[norm, i]
                    if n >= 2:
                        act.wait_ge(ms_done[part], n - 1)
                    c = NT * norm + i
                    nc.scalar.activation(sq_sink[:], src, ACT.Square, scale=D ** -0.5,
                                         accum_out=ms[:, c:c + 1]).then_inc(ms_done[part], 1)

                def split_hi(j):
                    part = j >= N_PROJ
                    act.wait_ge(raw_loaded[part][j % 2], raw_landed(j))
                    if j < 2:
                        act.wait_ge(mm_done[1], LATE_EVENTS - 4 * (1 - j))
                    elif j < N_PROJ + 2:
                        act.wait_ge(mm_done[0], tiles_before(j - 1))
                    else:
                        act.wait_ge(mm_done[1], out_unit_end(j - 2 - N_PROJ))
                    nc.scalar.copy(w_hi[:, j % 2], raw[:, j % 2]).then_inc(hi_ready[part], 1)

                def split_hi_mlp(g, jj):
                    act.wait_ge(raw_loaded[1][jj % 2], g * 64 + (RAW_OUT + 16 * (jj // 2 + 1)))
                    act.wait_ge(mm_done[1], unit_end(g, jj - 2))
                    nc.scalar.copy(w_hi[:, jj % 2], raw[:, jj % 2]).then_inc(hi_ready[1], 1)

                def norm_hi(stage, i):
                    for c in range(2):
                        act.wait_ge(nt_done[stage], 2 * i + c + 1)
                        nc.scalar.copy(hT_hi[:, 4 * c:4 * c + 4, i * P:(i + 1) * P],
                                       ps[:, 2 * i + c, :].rearrange("p (k t) -> p k t", k=4)).then_inc(nhi_done[stage], 1)

                for i in range(NT):
                    act.wait_ge(x_loaded[i], 16)
                    act.wait_ge(applied, NT + i + 1)
                    mean_square(0, i, X[:, i])
                    if i == 0:
                        split_hi(0)
                    elif i < NT - 1:
                        norm_hi(0, i - 1)
                split_hi(1)
                norm_hi(0, NT - 2)
                def tile_copy(j, t):
                    kind, col = UNITS[j]
                    x = tiles_before(j) + t
                    act.wait_ge(mm_done[0], x + 1)
                    if kind == "t":
                        src = ps[:, x % 2, 0:256]
                        if col in (C_MLV, C_MLV + 256):
                            h = (col - C_MLV) // ML_DV
                            ins = nc.scalar.copy(ml_v[:, t, h:h + 2, 0:ML_DV], src.rearrange("p (h e) -> p h e", h=2))
                        elif col in (C_MLO, C_MLO + 256):
                            ins = nc.scalar.copy(ml_gate[:, t, col - C_MLO:col - C_MLO + 256], src)
                        else:
                            h = HEADS * (col == C_DSV)
                            ins = nc.scalar.copy(sm_v[:, t, h:h + HEADS], src.rearrange("p (h e) -> p h e", h=HEADS))
                    else:
                        src = ps[:, x % 2, :]
                        if kind == "small":
                            nc.scalar.copy(rows[0:36, :], src[DK:DK + 36, :])
                            nc.scalar.copy(ix_k[0:DK, :], src[0:DK, :])
                            ins = nc.scalar.copy(ix_k[DK:2 * DK, :], src[0:DK, :])
                        elif col in (C_MLQ, C_MLK):
                            if col == C_MLQ:
                                act.wait_ge(conv_step, 4 * (t + 1))
                            ins = nc.scalar.copy(conv_in[:, t], src)
                        else:
                            dst, at = {C_IXQ: (ix_q, 0), C_MBQ: (sm_qk[0], 0), C_MBK: (sm_qk[0], 2),
                                       C_DSQ: (sm_qk[1], 0), C_DSK: (sm_qk[1], 2)}[col]
                            ins = nc.scalar.copy(dst[:, at + t], src)
                    ins.then_inc(tile_out, 1)

                tile_copy(0, 0)
                norm_hi(0, NT - 1)
                act.sem_inc(part_over[1], 1)

                def index_relu(n):
                    j, h = n // HEADS + 1, n % HEADS
                    act.wait_ge(idx_done, n + 1)
                    if n >= 2:
                        act.wait_ge(idx_acc, n - 1)
                    nc.scalar.activation(relu_s[:, n % 2, :(j + 1) * P], ps[:, 2 + n % 2, :(j + 1) * P],
                                         ACT.Relu).then_inc(idx_relu, 1)

                def gate(t):
                    act.wait_ge(tile_out, tiles_before(N_PROJ - 1) + t + 1)
                    nc.scalar.activation(ml_gate[:, t], ml_gate[:, t], ACT.Sigmoid).then_inc(gate_done, 1)

                def decay(n):
                    j, h = divmod(n, HEADS)
                    if n == 0:
                        act.wait_ge(m_spread, 16 * HEADS)
                        act.wait_ge(cols_done, 4)
                    if n >= 2:
                        act.wait_ge(ml_p, n - 1)
                    diag = sbuf_s[:, n % 2, j * P:(j + 1) * P]
                    nc.scalar.activation(diag, m_all[:, j, h, :], ACT.Relu,
                                         bias=a_neg[:, j, h:h + 1]).then_inc(decay_arg, 1)
                    for i in range(j):
                        nc.scalar.activation(sbuf_s[:, n % 2, i * P:(i + 1) * P], m_all[:, j, h, :], ACT.Exp,
                                             bias=a_col[:, i, h:h + 1], scale=-1.0)
                    act.wait_ge(decay_arg, n + 1)
                    ins = nc.scalar.activation(diag, diag, ACT.Exp, scale=-1.0)
                    ins.then_inc(decay_done, 1)

                def sm_exp(m):
                    k, h = divmod(m, HEADS)
                    w = (k % NT + 1) * P
                    act.wait_ge(sm_masked, m + 1)
                    if m >= 2:
                        act.wait_ge(pt_done, m - 1)
                    if h == 0 and k >= 2:
                        act.wait_ge(rsum_done, k - 1)
                    nc.scalar.activation(sbuf_p[:, m % 2, :w], sbuf_s[:, m % 2, :w], ACT.Exp,
                                         bias=nmin[:, m % 2:m % 2 + 1], scale=-1.0,
                                         accum_out=sums[:, k % 2, h:h + 1]).then_inc(exp_done, 1)

                def pt_copy(m):
                    w = (m // HEADS % NT + 1) * P
                    act.wait_ge(pt_done, m + 1)
                    if m >= 2:
                        act.wait_ge(pv_done, m - 1)
                    nc.scalar.copy(sbuf_pt[:, m % 2, :w], ps[:, 4 + m % 2, :w]).then_inc(pt_out, 1)

                def head_step(n):
                    if n < N_ML:
                        decay(n)
                    elif n < N_TASKS:
                        sm_exp(n - N_ML)
                    if N_ML < n <= N_TASKS:
                        pt_copy(n - 1 - N_ML)
                    if n >= N_TASKS:
                        for t in ((0, 1), (2,))[n - N_TASKS]:
                            gate(t)

                for j in range(IDX_FROM):
                    for t in range(j == 0, tiles_of(j)):
                        tile_copy(j, t)
                    split_hi(j + 2)
                    if j == 2:
                        act.wait_ge(tile_out, tiles_before(3))
                        nc.scalar.copy(rows_t[0:2 * HEADS, :], rows[0:2 * HEADS, :]).then_inc(iw_copied, 1)
                        act.wait_ge(gate_step, 2)
                        nc.scalar.activation(g_n, g_n, ACT.Exp).then_inc(softplus_done, 1)
                        act.wait_ge(softplus_done, 1)
                        nc.scalar.activation(g_n, g_n, ACT.Ln, bias=1.0).then_inc(softplus_done, 1)
                for j in range(IDX_FROM, N_PROJ):
                    for part in range(PARTS):
                        for t in tiles_in_part(j, part):
                            tile_copy(j, t)
                        if part == PARTS - 1:
                            if j == N_PROJ - 2:
                                begin(act, 1, l)
                            if HEAD_FROM <= j < N_PROJ - 1:
                                split_hi(j + 2)
                        for o, at in enumerate(SILU_AT):
                            if at == (j, part):
                                act.wait_ge(conv_step, 4 * (o + 1))
                                nc.scalar.activation(ml_qk[:, CONV_CHUNK[o]], conv_acc[:, o % 2],
                                                     ACT.Silu).then_inc(silu_done, 1)
                        if j < HEAD_FROM:
                            index_relu((j - IDX_FROM) * PARTS + part)
                            if part == PARTS - 1:
                                split_hi(j + 2)
                            if (j, part) == (IDX_FROM, 1):
                                act.wait_ge(rows_turned, 1)
                                r = ps[:, 4, 0:NT * 36].rearrange("p (t c) -> p t c", t=NT)
                                nc.scalar.copy(a_col[:], r[:, :, 0:HEADS]).then_inc(cols_done, 1)
                                nc.scalar.mul(a_neg[:], r[:, :, 0:HEADS], -1.0).then_inc(cols_done, 1)
                                nc.scalar.mul(iw_col[:], r[:, :, HEADS:2 * HEADS],
                                              (HEADS * DK) ** -0.5).then_inc(cols_done, 1)
                                nc.scalar.activation(expm[:], r[:, :, 32:32 + HEADS], ACT.Exp,
                                                     scale=-1.0).then_inc(cols_done, 1)
                        else:
                            for n in steps_of(j, part):
                                head_step(n)
                gate(NT - 1)
                for at, n in enumerate(TURNS):
                    c, i = divmod(n, NT)
                    act.wait_ge(nt_done[0], 8 + at + 1)
                    nc.scalar.copy(hT_hi[:, 4 * c:4 * c + 4, i * P:(i + 1) * P],
                                   ps[:, n, :].rearrange("p (k t) -> p k t", k=4)).then_inc(nhi_done[0], 1)
                    if n == 1:
                        split_hi(N_PROJ + 1)
                act.sem_inc(part_over[0], 1)
                split_hi(N_PROJ + 2)
                split_hi(N_PROJ + 3)
                nc.scalar.activation(table_sink[:], half[:, 0:1], ACT.Exp).then_inc(table_back, 1)

                def mix_square(i):
                    act.wait_ge(mm_done[1], out_event(N_OUT - 1, i))
                    mean_square(1, i, ps[:, 2 * i:2 * i + 2, :].rearrange("p a b -> p (a b)"))

                def x_square(i):
                    act.wait_ge(applied, i + 1)
                    mean_square(2, i, X[:, i])

                mix_square(0)
                mix_square(1)
                x_square(0)
                x_square(1)
                act.wait_ge(raw_loaded[1][0], RAW_OUT + 16)
                act.wait_ge(mm_done[1], out_unit_end(2))
                nc.scalar.copy(w_hi[:, 0], raw[:, 0]).then_inc(hi_ready[1], 1)
                norm_hi(1, 0)
                mix_square(2)
                norm_hi(1, 1)
                mix_square(3)
                x_square(2)
                x_square(3)
                norm_hi(1, 2)
                norm_hi(1, 3)
                split_hi_mlp(0, 1)

                def hidden(g, m):
                    act.wait_ge(mm_done[1], mlp_event(g, m // 2, m % 2))
                    act.wait_ge(hid_ready, g * HID + m + 1)
                    nc.scalar.activation(hid_r[:, m % 2], ps[:, m, :], ACT.Relu).then_inc(hid_relu, 1)
                    act.wait_ge(hid_relu, g * HID + m + 1)
                    nc.scalar.activation(hid_hi[:, m], hid_r[:, m % 2], ACT.Square).then_inc(hid_hi_done, 1)

                def group(g, is_last):
                    for jj in range(GU):
                        if jj < 4:
                            hidden(g, 2 * jj)
                            hidden(g, 2 * jj + 1)
                        if jj + 2 < GU:
                            split_hi_mlp(g, jj + 2)
                        elif not is_last:
                            split_hi_mlp(g + 1, jj + 2 - GU)

                with act.Fori(0, GROUPS - 1) as g:
                    group(g, False)
                group(GROUPS - 1, True)
                for i in range(NT):
                    act.wait_ge(y_out, 8 * GROUPS + 8 + i - 3)
                    mean_square(3, i, Y[:, i])
                act.wait_ge(ms_done[1], len(NORMS[1]))
                act.wait_ge(table_back, 1)

        @block.vector
        def _(dve):
            with dve.Fori(0, DEPTH) as l:
                begin(dve, 0, l)

                def split_lo_at(part, n, j):
                    dve.wait_ge(hi_ready[part], n + 1)
                    nc.vector.tensor_tensor(w_lo[:, j % 2], raw[:, j % 2], w_hi[:, j % 2].bitcast(F32),
                                            ALU.subtract).then_inc(lo_ready[part], 1)

                def split_lo(j):
                    split_lo_at(j >= N_PROJ, j - N_PROJ * (j >= N_PROJ), j)

                def normed(norm, i):
                    part = NORM_PART[norm, i]
                    dve.wait_ge(rstd_done[part], NORM_AT[norm, i])
                    dve.wait_ge(gain_pre_loaded[part], 16)
                    c = NT * norm + i
                    nc.vector.scalar_tensor_tensor(Y[:, i], X[:, i], rstd[:, c:c + 1], gain_pre[:], ALU.mult,
                                                   ALU.mult).then_inc(xn_done[part], 1)

                def norm_lo(stage, i):
                    for c in range(2):
                        dve.wait_ge(nhi_done[stage], 2 * i + c + 1)
                        nc.vector.tensor_tensor(
                            hT_lo[:, 4 * c:4 * c + 4, i * P:(i + 1) * P],
                            ps[:, 2 * i + c, :].rearrange("p (k t) -> p k t", k=4),
                            hT_hi[:, 4 * c:4 * c + 4, i * P:(i + 1) * P].bitcast(F32),
                            ALU.subtract).then_inc(nlo_done[stage], 1)

                def gain_on(norm, i, src, dst):
                    dve.wait_ge(gain_post_loaded, 16 if norm == 1 else 32)
                    nc.vector.tensor_tensor(dst, src, gain_post[:], ALU.mult).then_inc(applied_t, 1)

                def apply(norm, i, src):
                    n = i + 1 + (NT if norm == 3 else 0)
                    c = NT * norm + i
                    dve.wait_ge(rstd_done[1], NORM_AT[norm, i])
                    dve.wait_ge(applied_t, n)
                    nc.vector.scalar_tensor_tensor(X[:, i], src, rstd[:, c:c + 1], X[:, i], ALU.mult,
                                                   ALU.add).then_inc(applied, 1)

                dve.wait_ge(applied, 2 * NT)
                for i in range(NT):
                    normed(0, i)
                    if i == 0:
                        split_lo(0)
                    else:
                        norm_lo(0, i - 1)
                split_lo(1)
                norm_lo(0, NT - 1)
                dve.sem_inc(part_over[1], 1)

                def conv(o):
                    chunk = CONV_CHUNK[o]
                    acc, src = conv_acc[:, o % 2], conv_in[:, o % 2]
                    dve.wait_ge(tile_out, tiles_before(4) + o + 1)
                    dve.wait_ge(conv_w_ready, 1)
                    if o >= 2:
                        dve.wait_ge(silu_done, o - 1)
                    for n, k in enumerate((3, 2, 1, 0)):
                        w = conv_w[:, 4 * k + chunk:4 * k + chunk + 1]
                        d = 3 - k
                        if n == 0:
                            ins = nc.vector.tensor_scalar(acc, src, w, None, ALU.mult)
                        else:
                            dve.wait_ge(conv_step, 4 * o + n)
                            ins = nc.vector.scalar_tensor_tensor(acc[:, d:], src[:, :SEQ - d], w, acc[:, d:],
                                                                 ALU.mult, ALU.add)
                        ins.then_inc(conv_step, 1)

                def gates_f():
                    dve.wait_ge(params_loaded, 64)
                    dve.wait_ge(tile_out, tiles_before(3))
                    nc.vector.tensor_scalar(g_f, rows[32:32 + HEADS, :], gate_bias[32:32 + HEADS, :], None,
                                            ALU.add).then_inc(gate_step, 1)
                    dve.wait_ge(gate_step, 1)
                    nc.vector.scalar_tensor_tensor(g_n, g_f, -1.0, g_f, ALU.mult, ALU.min).then_inc(gate_step, 1)

                def gates_scan():
                    dve.wait_ge(softplus_done, 2)
                    nc.vector.scalar_tensor_tensor(g_f, g_f, 0.0, g_n, ALU.min, ALU.subtract).then_inc(gate_step, 1)
                    dve.wait_ge(gate_step, 3)
                    nc.vector.tensor_tensor_scan(g_B, ones[:], g_f, 0.0, ALU.mult, ALU.add).then_inc(gate_step, 1)
                    dve.wait_ge(gate_step, 4)
                    dve.wait_ge(iw_copied, 1)
                    nc.vector.scalar_tensor_tensor(rows_t[0:HEADS, :], rows[0:HEADS, :], gate_bias[0:HEADS, :], g_B,
                                                   ALU.add, ALU.subtract).then_inc(gate_step, 1)
                    dve.wait_ge(gate_step, 5)
                    nc.vector.tensor_tensor_scan(g_M, rows_t[0:HEADS, :], rows_t[0:HEADS, :], 0.0, ALU.max,
                                                 ALU.max).then_inc(gate_step, 1)
                    dve.wait_ge(gate_step, 6)
                    nc.vector.tensor_tensor(rows_t[32:32 + HEADS, :], g_B, g_M, ALU.add).then_inc(gate_step, 1)

                def index_sum(n):
                    j, h = n // HEADS + 1, n % HEADS
                    w = (j + 1) * P
                    acc = score[:, SCORE_AT[j]:SCORE_AT[j] + w]
                    dve.wait_ge(idx_relu, n + 1)
                    if h == 0:
                        dve.wait_ge(cols_done, 3)
                        ins = nc.vector.tensor_scalar(acc, relu_s[:, n % 2, :w], iw_col[:, j, h:h + 1], None, ALU.mult)
                    else:
                        dve.wait_ge(idx_acc, n)
                        ins = nc.vector.scalar_tensor_tensor(acc, relu_s[:, n % 2, :w], iw_col[:, j, h:h + 1], acc,
                                                             ALU.mult, ALU.add)
                    ins.then_inc(idx_acc, 1)

                ROUNDS = TOPK // 8
                STEPS = 2 * ROUNDS + 2

                def topk(r):
                    j, r = divmod(r, ROUNDS)
                    j += 1
                    sc = score[:, SCORE_AT[j]:SCORE_AT[j] + (j + 1) * P]
                    at = STEPS * (j - 1) + 2 * r
                    if r == 0:
                        dve.wait_ge(score_ready, j)
                    if at:
                        dve.wait_ge(tk, at)
                    nc.vector.max(top8[:], sc).then_inc(tk, 1)
                    dve.wait_ge(tk, at + 1)
                    nc.vector.match_replace(sc, top8[:], sc, TAKEN).then_inc(tk, 1)
                    if r == ROUNDS - 1:
                        dve.wait_ge(tk, at + 2)
                        nc.vector.tensor_scalar(sc, sc, TAKEN, None, ALU.is_equal).then_inc(tk, 1)
                        dve.wait_ge(tk, at + 3)
                        nc.vector.tensor_scalar(sc, sc, -MASKED, MASKED, ALU.mult, ALU.add).then_inc(tk, 1)

                def ml_probs(n):
                    w = (n // HEADS + 1) * P
                    dve.wait_ge(st_done, n + 1)
                    dve.wait_ge(decay_cut, n + 1)
                    if n >= 2:
                        dve.wait_ge(ml_pv, n - 1)
                    nc.vector.scalar_tensor_tensor(sbuf_pt[:, n % 2, :w], ps[:, 2 + n % 2, :w], DK ** -0.5,
                                                   sbuf_s[:, n % 2, :w], ALU.mult, ALU.mult).then_inc(ml_p, 1)

                def ml_divide(p):
                    j, a = p // 2, 2 * (p % 2)
                    o = ps[:, 6 + p % 2, 0:2 * (ML_DV + 1)].rearrange("p (h e) -> p h e", h=2)
                    y = Y[:, j, a * ML_DV:(a + 2) * ML_DV].rearrange("p (h e) -> p h e", h=2)
                    d, r = den[:, j, a:a + 2], rden[:, j, a:a + 2]
                    dve.wait_ge(ml_pv, 2 * (p + 1))
                    nc.vector.scalar_tensor_tensor(d, o[:, :, ML_DV], -1.0, expm[:, j, a:a + 2], ALU.mult,
                                                   ALU.max).then_inc(ml_step, 1)
                    dve.wait_ge(ml_step, 4 * p + 1)
                    nc.vector.tensor_tensor(d, o[:, :, ML_DV], d, ALU.max).then_inc(ml_step, 1)
                    dve.wait_ge(ml_step, 4 * p + 2)
                    nc.vector.reciprocal(r, d).then_inc(ml_step, 1)
                    dve.wait_ge(ml_step, 4 * p + 3)
                    nc.vector.tensor_tensor(y, o[:, :, 0:ML_DV], r[:, :, None].to_broadcast([P, 2, ML_DV]),
                                            ALU.mult).then_inc(ml_fin, 1)
                    dve.wait_ge(ml_fin, p + 1)
                    if p:
                        dve.wait_ge(hms_done, p)
                    nc.vector.tensor_tensor(sq[:].rearrange("p (h e) -> p h e", h=2), y, y, ALU.mult).then_inc(ml_step, 1)
                    dve.wait_ge(ml_step, 4 * p + 4)
                    nc.vector.tensor_reduce(hms[:, j, a:a + 2], sq[:].rearrange("p (h e) -> p h e", h=2), AX.X,
                                            ALU.add).then_inc(hms_done, 1)

                def ml_gated(j):
                    dve.wait_ge(hrstd_done, 2 * (j + 1))
                    dve.wait_ge(ml_gained, 2 * (j + 1))
                    dve.wait_ge(gate_done, j + 1)
                    for h in range(HEADS):
                        y = Y[:, j, h * ML_DV:(h + 1) * ML_DV]
                        ins = nc.vector.scalar_tensor_tensor(y, y, hrstd[:, j, h:h + 1],
                                                             ml_gate[:, j, h * ML_DV:(h + 1) * ML_DV], ALU.mult,
                                                             ALU.mult)
                    ins.then_inc(ml_out, 1)

                def sm_mask(m):
                    grp, j = divmod(m // HEADS, NT)
                    w = (j + 1) * P
                    dve.wait_ge(sc_done, m + 1)
                    if m >= 2:
                        dve.wait_ge(exp_done, m - 1)
                    if grp == 1 and j:
                        dve.wait_ge(tk, STEPS * j)
                    nc.vector.tensor_tensor_reduce(sbuf_s[:, m % 2, :w], ps[:, 2 + m % 2, :w], mask_of(grp, j),
                                                   -DK ** -0.5, 3e38, ALU.add, ALU.min,
                                                   nmin[:, m % 2:m % 2 + 1]).then_inc(sm_masked, 1)

                def sm_divide(k):
                    grp, j = divmod(k, NT)
                    dve.wait_ge(pv_done, HEADS * (k + 1))
                    nc.vector.reciprocal(rsum[:, k % 2], sums[:, k % 2]).then_inc(rsum_done, 1)
                    dve.wait_ge(rsum_done, k + 1)
                    c = W_V + grp * W_SM
                    nc.vector.tensor_tensor(Y[:, j, c:c + W_SM].rearrange("p (h e) -> p h e", h=HEADS),
                                            ps[:, 6 + k % 2, 0:W_SM].rearrange("p (h e) -> p h e", h=HEADS),
                                            rsum[:, k % 2][:, :, None].to_broadcast([P, HEADS, DK]),
                                            ALU.mult).then_inc(sm_fin, 1)

                def head_step(n):
                    if N_ML <= n < N_TASKS:
                        sm_mask(n - N_ML)
                    if 1 <= n <= N_ML:
                        ml_probs(n - 1)
                    if n % 2 == 0 and 4 <= n <= N_ML + 2:
                        ml_divide((n - 4) // 2)
                    if n % HEADS == 2 and n >= N_ML + 6:
                        sm_divide((n - N_ML - 6) // HEADS)
                    if n < 3 * ROUNDS - AHEAD:
                        topk(n + AHEAD)
                    if n == N_TASKS + 1:
                        ml_gated(0)
                        ml_gated(1)

                for j in range(IDX_FROM):
                    if j == 0:
                        dve.wait_ge(conv_t, 1)
                        nc.vector.tensor_copy(conv_w[:], ps[:, 4, 0:16]).then_inc(conv_w_ready, 1)
                    split_lo(j + 2)
                    if j == 2:
                        gates_f()
                        gates_scan()
                for j in range(IDX_FROM, N_PROJ):
                    for part in range(PARTS):
                        if (j, part) in CONV_AT:
                            conv(CONV_AT.index((j, part)))
                        if part == (4 if j == HEAD_FROM else 0) and j > IDX_FROM:
                            if j + 1 == N_PROJ:
                                begin(dve, 1, l)
                            split_lo(j + 1)
                        if j < HEAD_FROM:
                            index_sum((j - IDX_FROM) * PARTS + part)
                            if j == HEAD_FROM - 1 and part < AHEAD:
                                topk(part)
                        else:
                            for n in steps_of(j, part):
                                head_step(n)
                sm_divide(2 * NT - 1)

                for at, n in enumerate(TURNS):
                    c, i = divmod(n, NT)
                    if n == 4:
                        ml_gated(2)
                        ml_gated(3)
                    dve.wait_ge(nhi_done[0], 8 + at + 1)
                    nc.vector.tensor_tensor(
                        hT_lo[:, 4 * c:4 * c + 4, i * P:(i + 1) * P], ps[:, n, :].rearrange("p (k t) -> p k t", k=4),
                        hT_hi[:, 4 * c:4 * c + 4, i * P:(i + 1) * P].bitcast(F32), ALU.subtract).then_inc(nlo_done[0], 1)
                dve.sem_inc(part_over[0], 1)
                dve.wait_ge(lo_ready[1], 2)
                split_lo(N_PROJ + 2)
                split_lo(N_PROJ + 3)

                def mixed_gain(i):
                    dve.wait_ge(ms_done[1], NORM_AT[1, i])
                    gain_on(1, i, ps[:, 2 * i:2 * i + 2, :].rearrange("p a b -> p (a b)"), Y[:, i])

                def mixed(i):
                    apply(1, i, Y[:, i])

                for i in (0, 1):
                    mixed_gain(i)
                    mixed(i)
                normed(2, 0)
                normed(2, 1)
                norm_lo(1, 0)
                mixed_gain(2)
                mixed(2)
                norm_lo(1, 1)
                dve.sem_inc(y_out, 8)
                dve.sem_inc(hid_ready, 2)
                mixed_gain(3)
                mixed(3)
                normed(2, 2)
                normed(2, 3)
                norm_lo(1, 2)
                norm_lo(1, 3)
                dve.wait_ge(lo_ready[1], N_OUT + 1)
                split_lo(N_PRE + 1)
                dve.wait_ge(y_zero, NT)

                def hidden(g, m):
                    dve.wait_ge(hid_ready, g * HID + m + 1)
                    dve.wait_ge(hid_relu, g * HID + m + 1)
                    nc.vector.tensor_tensor(hid_h[:, m % 2], hid_r[:, m % 2], hid_r[:, m % 2],
                                            ALU.mult).then_inc(hid_sq, 1)
                    dve.wait_ge(hid_hi_done, g * HID + m + 1)
                    dve.wait_ge(hid_sq, g * HID + m + 1)
                    nc.vector.tensor_tensor(hid_lo[:, m], hid_h[:, m % 2], hid_hi[:, m].bitcast(F32),
                                            ALU.subtract).then_inc(hid_ready, 1)

                def y_add(g, c, i):
                    dve.wait_ge(mm_done[1], mlp_event(g, 5 + 2 * c, i))
                    dve.wait_ge(y_out, g * 8 + (4 * c + i + 1))
                    y = Y[:, i, c * 512:(c + 1) * 512]
                    nc.vector.tensor_tensor(y, y, ps[:, 4 * c + i, :], ALU.add).then_inc(y_out, 1)

                def group(g, is_last):
                    for jj in range(GU):
                        if jj < 4:
                            hidden(g, 2 * jj)
                            hidden(g, 2 * jj + 1)
                        if jj + 2 < GU or not is_last:
                            split_lo_at(1, g * GU + (N_OUT + jj + 2), jj)
                        if jj == 5 or jj == 7 and not is_last:
                            for i in range(NT):
                                y_add(g, (jj - 5) // 2, i)

                with dve.Fori(0, GROUPS - 1) as g:
                    group(g, False)
                group(GROUPS - 1, True)
                dve.wait_ge(hid_ready, GROUPS * HID + 2)
                for i in range(NT):
                    y_add(GROUPS - 1, 1, i)
                    dve.wait_ge(y_out, 8 * GROUPS + 4 + i + 1)
                    if i >= 2:
                        dve.wait_ge(applied, NT + i - 1)
                    gain_on(3, i, Y[:, i], gained[i % 2])
                    if i:
                        apply(3, i - 1, gained[(i - 1) % 2])
                apply(3, NT - 1, gained[(NT - 1) % 2])
                dve.wait_ge(applied, 2 * NT)

        @block.tensor
        def _(pe):
            pe.wait_ge(const_step, 3)
            with pe.Fori(0, DEPTH) as l:
                begin(pe, 0, l)

                def turn(stage, i):
                    pe.wait_ge(xn_done[stage], i + 1)
                    if stage == 0:
                        pe.wait_ge(y_out, 8 * GROUPS + 2 * (i + 1))
                    for c in range(2):
                        for q in range(4):
                            k = 4 * c + q
                            ins = nc.tensor.transpose(ps[:, 2 * i + c, q * P:(q + 1) * P],
                                                      Y[:, i, k * P:(k + 1) * P], ident[:])
                        ins.then_inc(nt_done[stage], 1)

                def passes(o, st, mv, first, final):
                    nc.tensor.matmul(o, st[0], mv[1], start=first, stop=False)
                    nc.tensor.matmul(o, st[0], mv[0], start=False, stop=False)
                    return nc.tensor.matmul(o, st[1], mv[0], start=False, stop=final)

                def unit_part(j, part):
                    kind = UNITS[j][0]
                    hi, lo = slot(w_hi, j, "in"), slot(w_lo, j, "in")
                    n = tiles_of(j) * KD * 3 // PARTS
                    for at in range(part * n, (part + 1) * n):
                        t, k, which = at // (3 * KD), at // 3 % KD, at % 3
                        x = tiles_before(j) + t
                        if at == 0:
                            pe.wait_ge(lo_ready[0], j + 1)
                        if j == 0 and at % (3 * KD) == 0:
                            pe.wait_ge(nlo_done[0], 2 * (t + 1))
                        if at % (3 * KD) == 0 and x >= 2:
                            pe.wait_ge(tile_out, x - 1)
                        s = slice(t * P, (t + 1) * P)
                        first, final = at % (3 * KD) == 0, at % (3 * KD) == 3 * KD - 1
                        st_hi, st_lo = (hT_hi[:, k, s], hT_lo[:, k, s]) if kind == "t" else (hi[:, k, s], lo[:, k, s])
                        mv_hi, mv_lo = (hi[:, k, :], lo[:, k, :]) if kind == "t" else (hT_hi[:, k, :], hT_lo[:, k, :])
                        ins = nc.tensor.matmul(ps[:, x % 2, 0:256] if kind == "t" else ps[:, x % 2, :],
                                               st_lo if which == 2 else st_hi, mv_lo if which == 0 else mv_hi,
                                               start=first, stop=final)
                        if final:
                            ins.then_inc(mm_done[0], 1)

                def index_scores(n):
                    j, h = n // HEADS + 1, n % HEADS
                    if n == 0:
                        pe.wait_ge(tile_out, tiles_before(4))
                    if n >= 2:
                        pe.wait_ge(idx_relu, n - 1)
                    b = DK * (h % 2)
                    nc.tensor.matmul(ps[:, 2 + n % 2, :(j + 1) * P], ix_q[b:b + DK, h // 2, j * P:(j + 1) * P],
                                     ix_k[b:b + DK, :(j + 1) * P], start=True, stop=True).then_inc(idx_done, 1)

                def ml_scores(n):
                    j, h = divmod(n, HEADS)
                    b = DK * (h % 2)
                    if n in (0, 2):
                        pe.wait_ge(silu_done, 3 + n // 2)
                    if n < 2:
                        pe.wait_ge(idx_relu, N_IDX)
                    else:
                        pe.wait_ge(ml_p, n - 1)
                    for i in range(j + 1):
                        ins = nc.tensor.matmul(ps[:, 2 + n % 2, i * P:(i + 1) * P],
                                               ml_qk[b:b + DK, 2 + h // 2, i * P:(i + 1) * P],
                                               ml_qk[b:b + DK, h // 2, j * P:(j + 1) * P], start=True, stop=True)
                    ins.then_inc(st_done, 1)

                def ml_values(n):
                    j, h = divmod(n, HEADS)
                    p = n // 2
                    pe.wait_ge(ml_p, n + 1)
                    if n == 0:
                        pe.wait_ge(tile_out, tiles_before(HEAD_FROM))
                    if n % 2 == 0 and p >= 2:
                        pe.wait_ge(ml_fin, p - 1)
                    c = (ML_DV + 1) * (n % 2)
                    for i in range(j + 1):
                        ins = nc.tensor.matmul(ps[:, 6 + p % 2, c:c + ML_DV + 1],
                                               sbuf_pt[:, n % 2, i * P:(i + 1) * P], ml_v[:, i, h, :],
                                               start=(i == 0), stop=(i == j))
                    ins.then_inc(ml_pv, 1)

                def sm_scores(m):
                    k, h = divmod(m, HEADS)
                    grp, j = divmod(k, NT)
                    b = DK * (h % 2)
                    if m % N_ML == 0:
                        pe.wait_ge(tile_out, tiles_before(8 if grp == 0 else 11))
                    if m < 2:
                        pe.wait_ge(ml_p, N_ML - 1 + m)
                    else:
                        pe.wait_ge(sm_masked, m - 1)
                    nc.tensor.matmul(ps[:, 2 + m % 2, :(j + 1) * P], sm_qk[grp][b:b + DK, h // 2, j * P:(j + 1) * P],
                                     sm_qk[grp][b:b + DK, 2 + h // 2, :(j + 1) * P], start=True,
                                     stop=True).then_inc(sc_done, 1)

                def sm_turn(m):
                    j = m // HEADS % NT
                    pe.wait_ge(exp_done, m + 1)
                    if m < 2:
                        pe.wait_ge(cols_done, 4)
                    else:
                        pe.wait_ge(pt_out, m - 1)
                    for i in range(j + 1):
                        ins = nc.tensor.transpose(ps[:, 4 + m % 2, i * P:(i + 1) * P],
                                                  sbuf_p[:, m % 2, i * P:(i + 1) * P], ident[:])
                    ins.then_inc(pt_done, 1)

                def sm_values(m):
                    k, h = divmod(m, HEADS)
                    grp, j = divmod(k, NT)
                    pe.wait_ge(pt_out, m + 1)
                    if h == 0:
                        pe.wait_ge(tile_out, tiles_before(8 if grp == 0 else 11) + j + 1)
                        if k < 2:
                            pe.wait_ge(ml_fin, N_ML // 2 - 1 + k)
                        else:
                            pe.wait_ge(sm_fin, k - 1)
                    for i in range(j + 1):
                        ins = nc.tensor.matmul(ps[:, 6 + k % 2, h * DK:(h + 1) * DK],
                                               sbuf_pt[:, m % 2, i * P:(i + 1) * P],
                                               sm_v[:, i, HEADS * grp + h, :], start=(i == 0), stop=(i == j))
                    ins.then_inc(pv_done, 1)

                def head_step(n):
                    if n < N_ML:
                        ml_scores(n)
                    elif n < N_TASKS:
                        sm_scores(n - N_ML)
                    if N_ML < n <= N_TASKS:
                        sm_turn(n - 1 - N_ML)
                    if 2 <= n < N_ML + 2:
                        ml_values(n - 2)
                    elif n >= N_ML + 2:
                        sm_values(n - 2 - N_ML)

                pe.wait_ge(y_out, 8 * GROUPS + 4)
                for _ in range(WARM):
                    nc.tensor.transpose(ps[:, 3, 0:P], ident[:], ident[:])
                turn(0, 0)
                turn(0, 1)
                pe.wait_ge(const_step, 8)
                for j in range(IDX_FROM):
                    for part in range(PARTS):
                        unit_part(j, part)
                        if j == 0 and part in (1, 2):
                            turn(0, 1 + part)
                    if j == 0:
                        pe.wait_ge(mm_done[1], LATE_EVENTS)
                        pe.sem_inc(part_over[1], 1)
                        pe.wait_ge(params_loaded, 64)
                        pe.wait_ge(nlo_done[0], 8)
                        nc.tensor.transpose(ps[:, 4, 0:16], conv_rows[:], ident[0:16, 0:16]).then_inc(conv_t, 1)

                def turn_rows():
                    pe.wait_ge(gate_step, 7)
                    pe.wait_ge(iw_copied, 1)
                    pe.wait_ge(conv_w_ready, 1)
                    for t in range(NT):
                        ins = nc.tensor.transpose(ps[:, 4, t * 36:(t + 1) * 36],
                                                  rows_t[0:36, t * P:(t + 1) * P], ident[0:36, 0:36])
                    ins.then_inc(rows_turned, 1)

                for j in range(IDX_FROM, N_PROJ):
                    for part in range(PARTS):
                        unit_part(j, part)
                        if j < HEAD_FROM:
                            index_scores((j - IDX_FROM) * PARTS + part)
                            if (j, part) == (IDX_FROM, 1):
                                turn_rows()
                        else:
                            for n in steps_of(j, part):
                                head_step(n)

                def mix_turn(n):
                    c, i = divmod(n, NT)
                    for q in range(4):
                        k = 4 * c + q
                        ins = nc.tensor.transpose(ps[:, n, q * P:(q + 1) * P], Y[:, i, k * P:(k + 1) * P], ident[:])
                    ins.then_inc(nt_done[0], 1)

                def out_tile(j, t):
                    pe.wait_ge(lo_ready[1], j + 1 - N_PROJ)
                    hi, lo = slot(w_hi, j, "out"), slot(w_lo, j, "out")
                    s = slice(t * P, (t + 1) * P)
                    for c in range(2):
                        for k in range(2):
                            kk = 2 * (j - N_PROJ) + k
                            cs = slice(c * 512, (c + 1) * 512)
                            ins = passes(ps[:, 2 * t + c, :], (hT_hi[:, kk, s], hT_lo[:, kk, s]),
                                         (hi[:, k, cs], lo[:, k, cs]), kk == 0, kk == KD - 1)
                    ins.then_inc(mm_done[1], 1)

                pe.wait_ge(tile_out, PROJ_TILES)
                pe.wait_ge(sm_masked, N_SM)
                begin(pe, 1, l)
                order = iter(OUT_ORDER)

                def out_next(n):
                    for _ in range(n):
                        j, t = next(order)
                        out_tile(N_PROJ + j, t)

                for at, n in enumerate(TURNS):
                    if n < NT:
                        pe.wait_ge(ml_out, n + 1)
                    else:
                        pe.wait_ge(pt_out, N_SM)
                        pe.wait_ge(sm_fin, n + 1)
                    mix_turn(n)
                    if at == 3:
                        pe.wait_ge(nlo_done[0], 8 + 2)
                        out_next(1)
                pe.wait_ge(nlo_done[0], 8 + 6)
                out_next(2)
                pe.wait_ge(nlo_done[0], 8 + 2 * NT)
                out_next(1)
                pe.wait_ge(half_ready_out, 1)
                out_next(4)
                pe.sem_inc(part_over[0], 1)
                out_next(6)
                turn(1, 0)
                out_next(1)
                turn(1, 1)
                out_next(1)

                def ff1_tile(jj, t, cols, m):
                    hi, lo = slot(w_hi, jj, "in"), slot(w_lo, jj, "in")
                    s = slice(t * P, (t + 1) * P)
                    for k in range(KD):
                        ins = passes(ps[:, m, cols], (hi[:, k, s], lo[:, k, s]),
                                     (hT_hi[:, k, cols], hT_lo[:, k, cols]), k == 0, k == KD - 1)
                    return ins

                def ff1_unit(g, jj):
                    pe.wait_ge(lo_ready[1], g * GU + (N_OUT + jj + 1))
                    for t in range(2):
                        m = 2 * jj + t
                        pe.wait_ge(y_out, g * 8 + m + 1)
                        ff1_tile(jj, t, slice(0, SEQ), m).then_inc(mm_done[1], 1)

                def ff2_unit(g, jj):
                    c, kh = (jj - 4) // 2, jj % 2
                    hi, lo = slot(w_hi, jj, "t"), slot(w_lo, jj, "t")
                    pe.wait_ge(lo_ready[1], g * GU + (N_OUT + jj + 1))
                    if jj < 6:
                        pe.wait_ge(hid_ready, g * HID + (4 * kh + 4 + 2))
                    for t in range(NT):
                        s = slice(t * P, (t + 1) * P)
                        for k in range(4):
                            kk = 4 * kh + k
                            ins = passes(ps[:, 4 * c + t, :], (hid_hi[:, kk, s], hid_lo[:, kk, s]),
                                         (hi[:, k, :], lo[:, k, :]), kk == 0, kk == HID - 1)
                        ins.then_inc(mm_done[1], 1)

                def group(g, is_last):
                    for jj in range(1, GU):
                        if jj < 4:
                            ff1_unit(g, jj)
                        else:
                            ff2_unit(g, jj)
                    if not is_last:
                        ff1_unit(g + 1, 0)

                pe.wait_ge(half_ready_mlp, 1)
                pe.wait_ge(lo_ready[1], N_OUT + 1)
                pe.wait_ge(y_out, 2)
                pe.wait_ge(nlo_done[1], 4)
                for t in range(2):
                    ff1_tile(0, t, slice(0, 2 * P), t)
                turn(1, 2)
                turn(1, 3)
                pe.wait_ge(nlo_done[1], 8)
                for t in range(2):
                    ff1_tile(0, t, slice(2 * P, 4 * P), t).then_inc(mm_done[1], 1)
                with pe.Fori(0, GROUPS - 1) as g:
                    group(g, False)
                group(GROUPS - 1, True)


_INS = ["x", "norm_mix_pre", "w_in", "ml_conv", "ml_i_bias", "ml_f_bias", "ml_head_norm", "w_out",
        "norm_mix_post", "norm_mlp_pre", "w_ff1", "w_ff2", "norm_mlp_post"]


def kernel(**inputs):
    import numpy as np
    import concourse.bacc as bacc
    from concourse.bass_utils import run_bass_kernel_spmd

    nc = bacc.Bacc("TRN2", target_bir_lowering=False, num_devices=1)
    arrays, args = {}, []
    for name in _INS:
        a = np.ascontiguousarray(inputs[name])
        arrays[f"in_{name}"] = a
        args.append(nc.dram_tensor(f"in_{name}", a.shape, mybir.dt.from_np(a.dtype), kind="ExternalInput").ap())
    shape = (1, SEQ, D)
    args.append(nc.dram_tensor("out_x", shape, F32, kind="ExternalOutput").ap())
    trunk(nc, *args)
    r = run_bass_kernel_spmd(nc, [arrays], core_ids=[0])
    return r.results[0]["out_x"]
```
